# Optimizing a Trainium2 kernel written in Bass

```python
import jax, jax.numpy as jnp
from jax import lax
import numpy as np

D_MODEL = 1024
BATCH = 1
SEQ = 512
DEPTH = 2
DEC_BATCH = 8
DEC_SEQ = 16
PAST_LEN = 128

CHUNK = 64
GROUP_W = D_MODEL // 4
HEAD_DIM = 64
N_HEADS_G = GROUP_W // HEAD_DIM
POOL_WINDOWS = (2, 4, 8, 16)
POOL_GW = GROUP_W // len(POOL_WINDOWS)
POOL_STATE = max(POOL_WINDOWS) - 1
CONV_W = 3
RWKV_DECAY_RANK = 32
RWKV_A_RANK = 32
RWKV_GATE_RANK = 64
RWKV_IN = 3 * GROUP_W + RWKV_DECAY_RANK + RWKV_A_RANK + RWKV_GATE_RANK
RWKV_SPLITS = (GROUP_W, 2 * GROUP_W, 3 * GROUP_W, 3 * GROUP_W + RWKV_DECAY_RANK,
               3 * GROUP_W + RWKV_DECAY_RANK + RWKV_A_RANK)
POOL_IN = GROUP_W
CONV_IN = 3 * GROUP_W
SB_IN = 3 * GROUP_W
PROJ_IN = POOL_IN + RWKV_IN + CONV_IN + SB_IN
PROJ_SPLITS = (POOL_IN, POOL_IN + RWKV_IN, POOL_IN + RWKV_IN + CONV_IN)
D_FF = 256 * ((8 * D_MODEL // 3 + 255) // 256)
Q_BLOCK = 128
RMS_EPS = 1e-6
GN_EPS = 64e-5

kernel_name = 'hybrid_stream_encoder_step'

def rmsnorm(x, g):
    xf = x.astype(jnp.float32)
    y = xf * lax.rsqrt(jnp.mean(xf * xf, axis=-1, keepdims=True) + RMS_EPS)
    return (y * g.astype(jnp.float32)).astype(x.dtype)

def swiglu(x, w_gate, w_up, w_down):
    return (jax.nn.silu(x @ w_gate) * (x @ w_up)) @ w_down

def pool_mixer(u, prefix, pos, w_grp, scale):
    T = u.shape[1]
    full = jnp.concatenate([prefix.astype(u.dtype), u], axis=1)
    ff = full.astype(jnp.float32)
    cs = jnp.concatenate([jnp.zeros_like(ff[:, :1]), jnp.cumsum(ff, axis=1)], axis=1)
    end = cs[:, POOL_STATE + 1:]
    outs = []
    for gi, w in enumerate(POOL_WINDOWS):
        sl = slice(gi * POOL_GW, (gi + 1) * POOL_GW)
        start = cs[:, POOL_STATE + 1 - w: POOL_STATE + 1 - w + T, sl]
        cnt = jnp.minimum(w, pos + 1).astype(jnp.float32)[None, :, None]
        d = (end[..., sl] - start) / cnt - u[..., sl].astype(jnp.float32)
        outs.append(d @ w_grp[gi])
    y = jnp.concatenate(outs, axis=-1) * scale
    return y.astype(u.dtype), full[:, -POOL_STATE:]

def rwkv7_mixer(u, shift_prev, wkv_prev, mu, w0, w2, a0, a2, g2, k_k, k_a, r_k, ln_w, ln_b):
    B, T, _ = u.shape
    f32 = jnp.float32
    prev = jnp.concatenate([shift_prev[:, None, :].astype(u.dtype), u[:, :-1]], axis=1)
    xs = u + (prev - u) * mu
    r, k, v, dw, da, dg = jnp.split(xs, RWKV_SPLITS, axis=-1)
    w = -jax.nn.softplus(-(w0 + jnp.tanh(dw) @ w2).astype(f32)) - 0.5
    decay = jnp.exp(-jnp.exp(w))
    a = jax.nn.sigmoid((a0 + da @ a2).astype(f32))
    g = jax.nn.sigmoid(dg) @ g2
    heads = lambda t: t.reshape(B, T, N_HEADS_G, HEAD_DIM)
    kk = heads((k * k_k).astype(f32))
    kk = kk / jnp.maximum(jnp.sqrt(jnp.sum(kk * kk, axis=-1, keepdims=True)), 1e-12)
    kh = heads(k.astype(f32) * (1.0 + (a - 1.0) * k_a.astype(f32)))
    rh, vh, ah, wh = heads(r.astype(f32)), heads(v.astype(f32)), heads(a), heads(decay)

    def step(S, inp):
        r_t, w_t, k_t, v_t, kk_t, a_t = inp
        s_kk = jnp.einsum('bhvk,bhk->bhv', S, kk_t)
        S = (S * w_t[:, :, None, :] - s_kk[..., None] * (kk_t * a_t)[:, :, None, :]
             + v_t[..., None] * k_t[:, :, None, :])
        return S, jnp.einsum('bhvk,bhk->bhv', S, r_t)

    seq = tuple(jnp.moveaxis(t, 1, 0) for t in (rh, wh, kh, vh, kk, ah))
    S_T, ys = lax.scan(step, wkv_prev.astype(f32), seq)
    y = jnp.moveaxis(ys, 0, 1)
    mean = jnp.mean(y, axis=-1, keepdims=True)
    var = jnp.mean(jnp.square(y - mean), axis=-1, keepdims=True)
    y = ((y - mean) * lax.rsqrt(var + GN_EPS)).reshape(B, T, GROUP_W) * ln_w + ln_b
    bonus = jnp.sum(rh * kh * r_k.astype(f32), axis=-1, keepdims=True) * vh
    y = (y + bonus.reshape(B, T, GROUP_W)) * g
    return y.astype(u.dtype), u[:, -1], S_T

def conv_mixer(u, prefix, conv_w):
    T = u.shape[1]
    b, c, xin = jnp.split(u, 3, axis=-1)
    zf = jnp.concatenate([prefix.astype(u.dtype), c * xin], axis=1)
    y = zf[:, 0:T] * conv_w[0]
    for tap in range(1, CONV_W):
        y = y + zf[:, tap:tap + T] * conv_w[tap]
    return b * y, zf[:, -(CONV_W - 1):]

def sb_attend(q, k, v, q_pos, k_pos):
    z = jnp.einsum('bqhd,bshd->bhqs', q, k).astype(jnp.float32) * (HEAD_DIM ** -0.5)
    visible = k_pos[None, :] < q_pos[:, None]
    log_keep = jnp.where(visible, jax.nn.log_sigmoid(-z), 0.0)
    log_after = lax.cumsum(log_keep, axis=3, reverse=True) - log_keep
    attn = jnp.where(visible, jnp.exp(jax.nn.log_sigmoid(z) + log_after), 0.0)
    return jnp.einsum('bhqs,bshd->bqhd', attn, v.astype(jnp.float32))

def stick_breaking(q, k, v, q_pos, k_pos):
    B, T = q.shape[0], q.shape[1]
    if T <= Q_BLOCK:
        return sb_attend(q, k, v, q_pos, k_pos)
    nb = T // Q_BLOCK
    qb = jnp.moveaxis(q.reshape(B, nb, Q_BLOCK, N_HEADS_G, HEAD_DIM), 1, 0)
    pb = q_pos.reshape(nb, Q_BLOCK)
    ob = lax.map(lambda qp: sb_attend(qp[0], k, v, qp[1], k_pos), (qb, pb))
    return jnp.moveaxis(ob, 0, 1).reshape(B, T, N_HEADS_G, HEAD_DIM)

def trunk(x, k_past, v_past, wkv0, shift0, conv0, pool0, prm):
    B, T, _ = x.shape
    past = k_past.shape[2]
    q_pos = past + jnp.arange(T, dtype=jnp.int32)
    k_pos = jnp.arange(past + T, dtype=jnp.int32)
    ks, vs, wkvs, shifts, convs, pools = [], [], [], [], [], []
    for l in range(DEPTH):
        g = prm['norm_g'][l]
        h = rmsnorm(x, g[0])
        x = x + 0.5 * rmsnorm(swiglu(h, prm['ffn_w_gate'][l, 0], prm['ffn_w_up'][l, 0],
                                     prm['ffn_w_down'][l, 0]), g[1])
        h = rmsnorm(x, g[2])
        u = h @ prm['w_in'][l]
        u_pool, u_rwkv, u_conv, u_sb = jnp.split(u, PROJ_SPLITS, axis=-1)
        y_pool, pool_new = pool_mixer(u_pool, pool0[l], q_pos, prm['pool_w'][l], prm['pool_scale'][l])
        y_rwkv, shift_new, wkv_new = rwkv7_mixer(
            u_rwkv, shift0[l], wkv0[l], prm['rwkv_mu'][l], prm['rwkv_w0'][l], prm['rwkv_w2'][l],
            prm['rwkv_a0'][l], prm['rwkv_a2'][l], prm['rwkv_g2'][l], prm['rwkv_k_k'][l],
            prm['rwkv_k_a'][l], prm['rwkv_r_k'][l], prm['rwkv_ln_w'][l], prm['rwkv_ln_b'][l])
        y_conv, conv_new = conv_mixer(u_conv, conv0[l], prm['conv_w'][l])
        q, k, v = [t.reshape(B, T, N_HEADS_G, HEAD_DIM) for t in jnp.split(u_sb, 3, axis=-1)]
        k_all = jnp.concatenate([k_past[l].astype(k.dtype), k], axis=1)
        v_all = jnp.concatenate([v_past[l].astype(v.dtype), v], axis=1)
        y_sb = stick_breaking(q, k_all, v_all, q_pos, k_pos).reshape(B, T, GROUP_W).astype(x.dtype)
        y = jnp.concatenate([y_pool, y_rwkv, y_conv, y_sb], axis=-1) @ prm['w_out'][l]
        x = x + rmsnorm(y, g[3])
        h = rmsnorm(x, g[4])
        x = x + 0.5 * rmsnorm(swiglu(h, prm['ffn_w_gate'][l, 1], prm['ffn_w_up'][l, 1],
                                     prm['ffn_w_down'][l, 1]), g[5])
        ks.append(k); vs.append(v); wkvs.append(wkv_new); shifts.append(shift_new)
        convs.append(conv_new); pools.append(pool_new)
    return (x, jnp.stack(ks), jnp.stack(vs), jnp.stack(wkvs), jnp.stack(shifts),
            jnp.stack(convs), jnp.stack(pools))

def setup_inputs(seed: int = 0) -> dict:
    key = jax.random.key(seed)
    kk = jax.random.split(key, 32)
    L, D, G, H, N = DEPTH, D_MODEL, GROUP_W, N_HEADS_G, HEAD_DIM

    def nrm(i, shape, s):
        return jax.random.normal(kk[i], shape, jnp.float32) * s

    return {
        'x_prompt': nrm(0, (BATCH, SEQ, D), 1.0),
        'x_sample': nrm(1, (DEC_BATCH, DEC_SEQ, D), 1.0),
        'cache_sb_k': nrm(2, (L, DEC_BATCH, PAST_LEN, H, N), 1.0),
        'cache_sb_v': nrm(3, (L, DEC_BATCH, PAST_LEN, H, N), 1.0),
        'state_wkv': nrm(4, (L, DEC_BATCH, H, N, N), 0.5),
        'state_shift': nrm(5, (L, DEC_BATCH, RWKV_IN), 1.0),
        'state_conv': nrm(6, (L, DEC_BATCH, CONV_W - 1, G), 1.0),
        'state_pool': nrm(7, (L, DEC_BATCH, POOL_STATE, G), 1.0),
        'norm_g': 1.0 + nrm(8, (L, 6, D), 0.05),
        'ffn_w_gate': nrm(9, (L, 2, D, D_FF), D ** -0.5),
        'ffn_w_up': nrm(10, (L, 2, D, D_FF), D ** -0.5),
        'ffn_w_down': nrm(11, (L, 2, D_FF, D), D_FF ** -0.5),
        'w_in': nrm(12, (L, D, PROJ_IN), D ** -0.5),
        'w_out': nrm(13, (L, D, D), D ** -0.5),
        'pool_w': nrm(14, (L, len(POOL_WINDOWS), POOL_GW, POOL_GW), POOL_GW ** -0.5),
        'pool_scale': 1.0 + nrm(15, (L, G), 0.1),
        'rwkv_mu': jax.random.uniform(kk[16], (L, RWKV_IN), jnp.float32),
        'rwkv_w0': jax.random.uniform(kk[17], (L, G), jnp.float32, -6.0, -1.0),
        'rwkv_w2': nrm(18, (L, RWKV_DECAY_RANK, G), 0.1),
        'rwkv_a0': nrm(19, (L, G), 0.1),
        'rwkv_a2': nrm(20, (L, RWKV_A_RANK, G), 0.1),
        'rwkv_g2': nrm(21, (L, RWKV_GATE_RANK, G), RWKV_GATE_RANK ** -0.5),
        'rwkv_k_k': 1.0 + nrm(22, (L, G), 0.1),
        'rwkv_k_a': 1.0 + nrm(23, (L, G), 0.1),
        'rwkv_r_k': nrm(24, (L, H, N), 0.1),
        'rwkv_ln_w': 1.0 + nrm(25, (L, G), 0.05),
        'rwkv_ln_b': nrm(26, (L, G), 0.02),
        'conv_w': nrm(27, (L, CONV_W, G), CONV_W ** -0.5),
    }

def reference(x_prompt, x_sample, cache_sb_k, cache_sb_v, state_wkv, state_shift, state_conv, state_pool,
              norm_g, ffn_w_gate, ffn_w_up, ffn_w_down, w_in, w_out, pool_w, pool_scale,
              rwkv_mu, rwkv_w0, rwkv_w2, rwkv_a0, rwkv_a2, rwkv_g2, rwkv_k_k, rwkv_k_a, rwkv_r_k,
              rwkv_ln_w, rwkv_ln_b, conv_w):
    prm = dict(norm_g=norm_g, ffn_w_gate=ffn_w_gate, ffn_w_up=ffn_w_up, ffn_w_down=ffn_w_down,
               w_in=w_in, w_out=w_out, pool_w=pool_w, pool_scale=pool_scale, rwkv_mu=rwkv_mu,
               rwkv_w0=rwkv_w0, rwkv_w2=rwkv_w2, rwkv_a0=rwkv_a0, rwkv_a2=rwkv_a2, rwkv_g2=rwkv_g2,
               rwkv_k_k=rwkv_k_k, rwkv_k_a=rwkv_k_a, rwkv_r_k=rwkv_r_k, rwkv_ln_w=rwkv_ln_w,
               rwkv_ln_b=rwkv_ln_b, conv_w=conv_w)
    B = x_prompt.shape[0]
    dt = x_prompt.dtype
    zk = jnp.zeros((DEPTH, B, 0, N_HEADS_G, HEAD_DIM), dt)
    z_wkv = jnp.zeros((DEPTH, B, N_HEADS_G, HEAD_DIM, HEAD_DIM), jnp.float32)
    z_shift = jnp.zeros((DEPTH, B, RWKV_IN), dt)
    z_conv = jnp.zeros((DEPTH, B, CONV_W - 1, GROUP_W), dt)
    z_pool = jnp.zeros((DEPTH, B, POOL_STATE, GROUP_W), dt)
    y_prompt, p_sb_k, p_sb_v, p_wkv, p_shift, p_conv, p_pool = trunk(
        x_prompt, zk, zk, z_wkv, z_shift, z_conv, z_pool, prm)
    y_sample, s_sb_k, s_sb_v, s_wkv, s_shift, s_conv, s_pool = trunk(
        x_sample, cache_sb_k, cache_sb_v, state_wkv, state_shift, state_conv, state_pool, prm)
    return (y_prompt, y_sample, p_sb_k, p_sb_v, p_wkv, p_shift, p_conv, p_pool,
            s_sb_k, s_sb_v, s_wkv, s_shift, s_conv, s_pool)


_drawn_inputs = setup_inputs


def setup_inputs(seed=0):
    import zlib

    import numpy as np

    out = dict(_drawn_inputs(seed))
    spreads = {}
    factors = {'rwkv_ln_w': 3.159, 'rwkv_ln_b': 7.579}
    for name, (base, spread) in spreads.items():
        noise = np.random.default_rng([zlib.crc32(name.encode()), seed]).standard_normal(out[name].shape)
        drawn = base * np.exp(spread * noise) if base else spread * noise
        out[name] = __import__('jax').numpy.asarray(drawn.astype(out[name].dtype))
    for name, factor in factors.items():
        out[name] = (out[name] * factor).astype(out[name].dtype)
    return out
```

```python
import math
from contextlib import ExitStack

import concourse.bass as bass
from concourse import mybir
from concourse.alu_op_type import AluOpType as ALU

F32 = mybir.dt.float32
F32R = mybir.dt.float32r
ACT = mybir.ActivationFunctionType

P = 128
DEPTH, D, TP, NSTR, TS, PAST = 2, 1024, 512, 8, 16, 128
T = TP + NSTR * TS
TT = T // P
PT = TP // P
HALF = T // 2
DC = D // P
G = D // 4
GC = G // P
NH, HD = 4, 64
FF = 2816
FT = FF // P
RANKS = (32, 32, 64)
RWKV_IN = 3 * G + sum(RANKS)
RC = RWKV_IN // P
POOL_ST, CONV_W = 15, 3
PROJ = G + RWKV_IN + 6 * G
SLOTS = 8
CH = 64
NCH = P // CH
DECAY = math.exp(-0.5)
EPS, GN_EPS = 1e-6, 64e-5

W_RWKV = [8, 4, 5, 2, 3, 6, 7]
W_SB = [15, 16, 17, 18, 19, 20]
W_CONV = [9, 10, 11, 12, 13, 14]
W_POOL = [0, 1]
W_TILES = W_RWKV + W_CONV + W_POOL + W_SB
NW = len(W_TILES)
STATES_AT, DECAY_AT, A_AT, GATE_AT, KK_AT, BONUS_AT, TAILS_AT = 1, 3, 5, 7, 9, 11, 17

DOWN_CUTS = [(0, 8), (8, 15), (15, 22)]
FFN_BLOCKS = FT + len(DOWN_CUTS) * DC // 2
MIX_BLOCKS = [(NW + 1) // 2 + DC // 2, NW // 2 + DC // 2]
LAYER_BLOCKS = [2 * FFN_BLOCKS + m for m in MIX_BLOCKS]

VEC = {}
for _n, _c in (("norm_g", 6 * DC), ("pool_scale", GC), ("mu", RC), ("w0", GC), ("a0", GC), ("k_k", GC),
               ("k_a", GC), ("r_k", GC), ("ln_w", GC), ("ln_b", GC), ("conv_w", CONV_W * GC)):
    VEC[_n] = (sum(c for _, c in VEC.values()), _c)
NV = sum(c for _, c in VEC.values())

CON = {}
for _n, _c in (("ident", P), ("ones", P), ("headones", P), ("see_prompt", P), ("see_sample", P),
               ("reset", T), ("icnt", GC * 16), ("iw", GC),
               ("tri_prompt", 2 * P), ("tri_sample", 2 * P), ("level1", P), ("levels", 6 * P),
               ("rowmask", NSTR)):
    CON[_n] = (sum(c for _, c in CON.values()), _c)
NCON = sum(c for _, c in CON.values())
KEPT = CON["reset"][0]


def constants(np):
    t = np.zeros((P, NCON), np.float32)

    def put(name, a):
        at, n = CON[name]
        t[:, at:at + n] = a.reshape(P, n)

    i, j = np.arange(P)[:, None], np.arange(P)[None, :]
    put("ident", (i == j) * 1.0)
    put("ones", np.ones((P, P)))
    put("headones", (i // HD == j // HD) * 1.0)
    put("see_prompt", np.where(j < i, 0.0, -1e30))
    put("see_sample", np.where((j < i) & (i // TS == j // TS), 0.0, -1e30))
    tok = np.arange(T)
    put("reset", np.tile(np.where(tok < TP, tok % CH != 0, (tok - TP) % TS != 0) * 1.0, (P, 1)))
    win = np.array([[2, 8], [4, 16]])[np.arange(P) // 64]
    put("iw", 1.0 / win)
    put("icnt", 1.0 / np.minimum(win[:, :, None], np.arange(16)[None, None, :] + 1))
    for name, b in (("tri_prompt", CH), ("tri_sample", TS)):
        same = i // b == j // b
        put(name, np.stack([(i < j) & same, (i <= j) & same], 1) * 1.0)
    put("level1", ((i // 2 == j // 2) & (i > j)) * 1.0)
    put("levels", np.stack([(i // (2 * b) == j // (2 * b)) & (i // b < j // b) for b in (1, 2, 4, 8, 16, 32)], 1) * 1.0)
    put("rowmask", (i // TS == np.arange(NSTR)[None, :]) * 1.0)
    return t


SAMPLE_LEVELS, PROMPT_LEVELS = 3, 5
UNITS = (PT + 1) * NH


def levels_before(l, tt):
    return l * (PT * PROMPT_LEVELS + SAMPLE_LEVELS) + tt * PROMPT_LEVELS


def inner_levels_before(l, tt):
    return l * (PT * (PROMPT_LEVELS - 1) + SAMPLE_LEVELS - 1) + tt * (PROMPT_LEVELS - 1)



def build(nc, io):
    es = ExitStack()
    with es:
        sems = {}

        def sem(name):
            if name not in sems:
                sems[name] = es.enter_context(nc.semaphore(name))
            return sems[name]

        def sb(name, shape, dt=F32, stack=es):
            return stack.enter_context(nc.sbuf_tensor(name, shape, dt))

        XT = sb("xT", [P, DC, T])
        RAW = [sb(f"w_raw{s}", [P, SLOTS, P]) for s in (0, 1)]
        WSP = [sb(f"w_split{s}", [P, 2, SLOTS, P], F32R) for s in (0, 1)]
        SCR = sb("scratch", [P, 2, T])
        ACC = sb("square_sums", [P, T])
        CONS = sb("consts", [P, KEPT])
        VROW = sb("vec_rows", [NV, P])
        LV = sb("layer_vecs", [P, NV])
        KA1 = sb("one_minus_k_a", [P, GC])
        COLS = sb("token_cols", [P, TT])
        EPSC = sb("eps_cols", [P, 3])
        SMALLW = sb("rank_weights", [P, G])
        scope = ExitStack()
        H = sb("h_split", [P, DC, 2, T], F32R, scope)
        scope.close()
        scope = ExitStack()
        Y = sb("y", [P, DC, T], stack=scope)
        scope.close()
        hold = sb("h_region", [P, 2 * DC * T])
        scope = ExitStack()
        HID = sb("hidden_split", [P, FT, 2, T], F32R, scope)
        scope.close()
        scope = ExitStack()
        IO = sb("token_rows", [P, TT, D], stack=scope)
        scope.close()
        scope = ExitStack()
        YM = sb("y_mixer", [P, DC, T], stack=scope)
        scope.close()
        mix = ExitStack()
        XS = sb("xs", [P, RC, T], stack=mix)
        SBQ = sb("sb_qkv", [P, 6, T], stack=mix)
        CS = sb("decay_sum", [P, GC, T], stack=mix)
        CSP = sb("decay_sum_before", [P, GC, T], stack=mix)
        BA = sb("kk_a", [P, GC, T], stack=mix)
        KK = sb("kk", [P, GC, T], stack=mix)
        GA = sb("gate", [P, GC, T], stack=mix)
        BV = sb("bonus_v", [P, GC, T], stack=mix)
        scope = ExitStack()
        RWP = sb("rw_prompt", [P, RC, 1 + TP], stack=scope)
        RWS = sb("rw_sample", [P, RC, NSTR, 1 + TS], stack=scope)
        PBP = sb("pool_prompt", [P, GC, POOL_ST + TP], stack=scope)
        PBS = sb("pool_sample", [P, GC, NSTR, POOL_ST + TS], stack=scope)
        CV = sb("conv_in", [P, 6, T], stack=scope)
        ZP = sb("z_prompt", [P, GC, 2 + TP], stack=scope)
        ZS = sb("z_sample", [P, GC, NSTR, 2 + TS], stack=scope)
        RESET = sb("reset", [P, T], stack=scope)
        ICNT = sb("inv_counts", [P, GC, 16], stack=scope)
        IW = sb("inv_windows", [P, GC], stack=scope)
        scope.close()
        scope = ExitStack()
        VT = sb("v_rows", [P, TT, G], stack=scope)
        VC = sb("v_cache", [P, NSTR, G], stack=scope)
        KC = sb("k_cache", [P, NSTR, G], stack=scope)
        KCT = sb("k_cacheT", [P, GC, NSTR, PAST], stack=scope)
        QM = sb("q_masked", [P, GC, NSTR * (P + TS)], stack=scope)
        KE = sb("keep", [P, 2, TP + 8], stack=scope)
        AT = sb("attnT", [P, 2, 4, P], stack=scope)
        scope.close()
        scope = ExitStack()
        LTG = sb("beta_scores", [P, NH, 2, P], stack=scope)
        KTG = sb("kappa_scores", [P, NH, 2, P], stack=scope)
        X = sb("inv", [P, NH, P], stack=scope)
        XTR = sb("invT", [P, NH, P], stack=scope)
        NT = sb("level_blocks", [P, 2, NH, P], stack=scope)
        T1 = sb("level_product", [P, NH, P], stack=scope)
        AR = sb("alpha_rho_by_head", [P, 2, GC, 2, P], stack=scope)
        AFS = sb("alpha", [P, 2, GC, P], stack=scope)
        RFS = sb("rho", [P, 2, GC, P], stack=scope)
        PCS = sb("chunk_decay", [P, 2, GC, NSTR], stack=scope)
        BK = sb("beta_kappa", [P, 2, GC, P], stack=scope)
        TOK = sb("beta_kappa_v_rows", [P, 3, G], stack=scope)
        MVS = sb("mv", [P, G], stack=scope)
        RH = sb("rhs", [P, G], stack=scope)
        NU = sb("minus_u", [P, G], stack=scope)
        ST = sb("state_prompt", [P, GC, P], stack=scope)
        STS = sb("state_sample", [P, NSTR, GC, P], stack=scope)
        TRI = sb("triangles", [P, 2, P], stack=scope)
        LEV1 = sb("level1_mask", [P, P], stack=scope)
        LEV = sb("level_masks", [P, 6, P], stack=scope)
        ROWM = sb("row_masks", [P, NSTR], stack=scope)
        scope.close()
        mix.close()

        IDENT = CONS[:, CON["ident"][0]:CON["ident"][0] + P]
        ONES = CONS[:, CON["ones"][0]:CON["ones"][0] + P]
        HEADS = CONS[:, CON["headones"][0]:CON["headones"][0] + P]
        SEE = [CONS[:, CON[n][0]:CON[n][0] + P] for n in ("see_prompt", "see_sample")]
        PS = es.enter_context(nc.psum_tensor("ps", [P, 8, 512], F32))
        PSF = PS[:].rearrange("p b n -> p (b n)")

        def pset(q):
            return PS[:, 2 * q:2 * q + 2, 0:HALF]

        def halves(ap):
            return ap.rearrange("p (a n) -> p a n", a=2)

        def vec(name, c):
            return LV[:, VEC[name][0] + c:VEC[name][0] + c + 1]

        SGB, HB = SCR[:, 0, :], SCR[:, 1, :]
        SQR = [SCR[:, 0, :], ACC[:, :]]
        STIN = BV[:].rearrange("p g t -> p (g t)")[:, 0:RWKV_IN]
        STIN2 = KK[:].rearrange("p g t -> p (g t)")
        PW = ACC[:, 0:2 * P].rearrange("p (g n) -> p g n", g=2)
        CVF = CV[:].rearrange("p s t -> p (s t)")
        TAIL = SCR[:].rearrange("p s t -> p (s t)")
        OUTS = RWP[:].rearrange("p c t -> p (c t)")
        KT = SCR[:].rearrange("p s t -> p (s t)").rearrange("p (i n) -> p i n", i=TT)
        KCF = KC[:].rearrange("p b n -> p (b n)")
        SIG = KCF[:, 0:2 * TP].rearrange("p (s n) -> p s n", s=2)
        AW = KCF[:, 2 * TP:4 * TP].rearrange("p (s n) -> p s n", s=2)
        EXPS = SCR[:].rearrange("p s t -> p (s t)")[:, 0:3 * G].rearrange("p (k g n) -> p k g n", k=3, g=GC)
        BP = SCR[:].rearrange("p s t -> p (s t)")[:, 3 * G:5 * G].rearrange("p (k g n) -> p k g n", k=2, g=GC)
        SBF = SBQ[:].rearrange("p s t -> p (s t)")
        SN = SBF[:, 0:NSTR * G].rearrange("p (b g n) -> p b g n", b=NSTR, g=GC)
        NM = SBF[:, NSTR * G:NSTR * G + 2 * 512].rearrange("p (k b n) -> p k b n", k=2, b=NSTR)

        block = es.enter_context(nc.Block())

        def base(l, s, seg):
            return l * LAYER_BLOCKS[s] + (0, FFN_BLOCKS, FFN_BLOCKS + MIX_BLOCKS[s])[seg]

        w_in_v = io["w_in"].rearrange("l (c p) n -> l p c n", p=P)
        w_out_v = io["w_out"].rearrange("l (c p) n -> l p c n", p=P)
        w_gu_v = [io[n].rearrange("l f (c p) n -> l f p c n", p=P) for n in ("ffn_w_gate", "ffn_w_up")]
        w_dn_v = io["ffn_w_down"].rearrange("l f (c p) n -> l f p c n", p=P)

        @block.sync
        def _(sp):
            def load_block(s, k, src, n=SLOTS):
                sp.wait_ge(sem(f"hi_ready{s}"), k + 1)
                sp.wait_ge(sem(f"lo_ready{s}"), k + 1)
                sp.sem_inc(sem("slot_seen"), 1)
                sp.dma_start(RAW[s][:, 0:n, :], src).then_inc(sem(f"raw_loaded{s}"), 16)

            def load_ffn(l, f):
                k0, k1 = base(l, 0, 2 * f), base(l, 1, 2 * f)
                with sp.Fori(0, FT) as j:
                    load_block(0, k0 + j, w_gu_v[0][l, f, :, :, bass.ds(j * P, P)])
                    load_block(1, k1 + j, w_gu_v[1][l, f, :, :, bass.ds(j * P, P)])
                with sp.Fori(0, DC // 2) as i:
                    for m in (0, 1):
                        for b, (r0, r1) in enumerate(DOWN_CUTS):
                            q = m * 3 + b
                            load_block(q % 2, base(l, q % 2, 2 * f) + FT + i * 3 + q // 2,
                                       w_dn_v[l, f, :, r0:r1, bass.ds((i * 2 + m) * P, P)], r1 - r0)

            sp.dma_start(CONS[:], io["consts"][:, 0:KEPT]).then_inc(sem("consts_loaded"), 16)
            for i in range(TT):
                src = io["x_prompt"][0, i * P:(i + 1) * P, :] if i < PT else io["x_sample"].rearrange("b t n -> (b t) n")
                sp.dma_start(IO[:, i, :], src).then_inc(sem(f"x_loaded{i}"), 16)

            with sp.Fori(0, DEPTH) as l:
                sp.wait_ge(sem("vec_ready"), l + 1)
                for name, (r, n) in VEC.items():
                    src = io["norm_g" if name == "norm_g" else ("rwkv_" + name if name not in ("pool_scale", "conv_w") else name)][l]
                    if name in ("norm_g", "conv_w"):
                        src = src.rearrange("s (c p) -> s c p", p=P).rearrange("s c p -> (s c) p")
                    elif name == "r_k":
                        src = src.rearrange("h n -> (h n)").rearrange("(c p) -> c p", p=P)
                    else:
                        src = src.rearrange("(c p) -> c p", p=P)
                    sp.dma_start(VROW[r:r + n, :], src).then_inc(sem("vec_loaded"), 16)
                r = 0
                for name, n in zip(("rwkv_w2", "rwkv_a2", "rwkv_g2"), RANKS):
                    sp.dma_start(SMALLW[r:r + n, :], io[name][l]).then_inc(sem("rank_loaded"), 16)
                    r += n
                load_ffn(l, 0)
                k0, k1 = base(l, 0, 1), base(l, 1, 1)
                for t, w in enumerate(W_TILES):
                    load_block(t % 2, (k0, k1)[t % 2] + t // 2, w_in_v[l, :, :, w * P:(w + 1) * P])
                    if t == 1:
                        sp.wait_ge(sem("y_added"), 1 + (l * 3 + 1) * DC)
                        sp.dma_start(STIN[0:NSTR, :], io["state_shift"][l]).then_inc(sem("state_loaded"), 16)
                        sp.dma_start(STIN2[0:2 * NSTR, 0:G], io["state_conv"][l].rearrange("b t n -> (b t) n")).then_inc(sem("state_loaded"), 16)
                        sp.dma_start(STIN2[0:POOL_ST * NSTR, G:2 * G], io["state_pool"][l].rearrange("b t n -> (b t) n")).then_inc(sem("state_loaded"), 16)
                        for dst, name in ((RESET[:], "reset"), (ICNT[:].rearrange("p g n -> p (g n)"), "icnt"), (IW[:], "iw")):
                            at, n = CON[name]
                            sp.dma_start(dst, io["consts"][:, at:at + n]).then_inc(sem("tables_loaded"), 16)
                    if t == 5:
                        sp.wait_ge(sem("poolw_zeroed"), l + 1)
                        for g in range(2):
                            for e in range(2):
                                sp.dma_start(PW[64 * e:64 * e + 64, g, 64 * e:64 * e + 64], io["pool_w"][l, 2 * g + e]).then_inc(sem("poolw_loaded"), 16)
                kb = ((NW + 1) // 2, NW // 2)
                for m in (0, 1):
                    load_block(m, (k0, k1)[m] + kb[m], w_out_v[l, :, :, m * P:(m + 1) * P])
                sp.wait_ge(sem("tails_out"), l + 1)
                sp.dma_start(io["p_shift"][l], OUTS[0:1, 0:RWKV_IN]).then_inc(sem("tails_stored"), 16)
                sp.dma_start(io["s_shift"][l], OUTS[1:1 + NSTR, 0:RWKV_IN]).then_inc(sem("tails_stored"), 16)
                sp.dma_start(io["p_conv"][l, 0], OUTS[0:2, 896:896 + G]).then_inc(sem("tails_stored"), 16)
                sp.dma_start(io["s_conv"][l].rearrange("b t n -> (b t) n"), OUTS[2:2 + 2 * NSTR, 896:896 + G]).then_inc(sem("tails_stored"), 16)
                sp.dma_start(io["s_pool"][l].rearrange("b t n -> (b t) n"), OUTS[0:NSTR * POOL_ST, 1152:1152 + G]).then_inc(sem("tails_stored"), 16)
                sp.dma_start(io["p_pool"][l, 0], OUTS[0:POOL_ST, 1408:1408 + G]).then_inc(sem("tails_stored"), 16)
                sp.wait_ge(sem("attn_region"), l + 1)
                sp.dma_start(KC[:], io["cache_sb_k"][l].rearrange("b s h n -> s b (h n)")).then_inc(sem("kc_loaded"), 16)
                sp.dma_start(VC[:], io["cache_sb_v"][l].rearrange("b s h n -> s b (h n)")).then_inc(sem("vc_loaded"), 16)
                sp.wait_ge(sem("kv_out"), (l + 1) * TT)
                for src, a, b in ((KT, "p_sb_k", "s_sb_k"), (VT, "p_sb_v", "s_sb_v")):
                    sp.dma_start(io[a][l, 0].rearrange("(i p) h n -> p i (h n)", p=P), src[:, 0:PT, :]).then_inc(sem("kv_stored"), 16)
                    sp.dma_start(io[b][l].rearrange("b t h n -> (b t) (h n)"), src[:, PT, :]).then_inc(sem("kv_stored"), 16)
                sp.wait_ge(sem("rule_region"), l + 1)
                for dst, name in ((TRI[:].rearrange("p a n -> p (a n)"), "tri_prompt"), (LEV1[:], "level1"),
                                  (LEV[:].rearrange("p a n -> p (a n)"), "levels"), (ROWM[:], "rowmask")):
                    at, n = CON[name]
                    sp.dma_start(dst, io["consts"][:, at:at + n]).then_inc(sem("masks_loaded"), 16)
                wkv_in = io["state_wkv"][l].rearrange("b (g e) v k -> e v b g k", e=2)
                for g in range(2):
                    for e in range(2):
                        sp.dma_start(SN[64 * e:64 * e + 64, :, g, 64 * e:64 * e + 64], wkv_in[e, :, :, g, :]).then_inc(sem("wkv_loaded"), 16)
                sp.wait_ge(sem("scores_masked"), l * TT + PT)
                at, n = CON["tri_sample"]
                sp.dma_start(TRI[:].rearrange("p a n -> p (a n)"), io["consts"][:, at:at + n]).then_inc(sem("sample_tri_loaded"), 16)
                sp.wait_ge(sem("prompt_state_out"), l + 1)
                for g in range(2):
                    for e in range(2):
                        sp.dma_start(io["p_wkv"][l, 0, 2 * g + e], ST[64 * e:64 * e + 64, g, 64 * e:64 * e + 64]).then_inc(sem("wkv_stored"), 16)
                sp.wait_ge(sem("sample_state_out"), l + 1)
                wkv_out = io["s_wkv"][l].rearrange("b (g e) v k -> e v b g k", e=2)
                for g in range(2):
                    for e in range(2):
                        sp.dma_start(wkv_out[e, :, :, g, :], SN[64 * e:64 * e + 64, :, g, 64 * e:64 * e + 64]).then_inc(sem("wkv_stored"), 16)
                for m in range(2, DC):
                    load_block(m % 2, (k0, k1)[m % 2] + kb[m % 2] + m // 2, w_out_v[l, :, :, m * P:(m + 1) * P])
                load_ffn(l, 1)
            for s in (0, 1):
                load_block(s, DEPTH * LAYER_BLOCKS[s], w_gu_v[0][0, 0, :, :, 0:P])
            for i in range(TT):
                sp.wait_ge(sem("out_rows"), i + 1)
                dst = io["y_prompt"][0, i * P:(i + 1) * P, :] if i < PT else io["y_sample"].rearrange("b t n -> (b t) n")
                sp.dma_start(dst, IO[:, i, :]).then_inc(sem("y_stored"), 16)
            sp.wait_ge(sem("tails_stored"), DEPTH * 6 * 16)
            sp.wait_ge(sem("kv_stored"), DEPTH * 4 * 16)
            sp.wait_ge(sem("wkv_stored"), DEPTH * 8 * 16)
            sp.wait_ge(sem("y_stored"), TT * 16)
            for s in (0, 1):
                sp.wait_ge(sem(f"raw_loaded{s}"), 16 * (DEPTH * LAYER_BLOCKS[s] + 1))

        @block.gpsimd
        def _(pool):
            def low(s, k):
                pool.wait_ge(sem(f"hi_ready{s}"), k + 2)
                nc.gpsimd.tensor_tensor(WSP[s][:, 1], RAW[s][:], WSP[s][:, 0].bitcast(F32), ALU.subtract).then_inc(sem(f"lo_ready{s}"), 1)

            for s in (0, 1):
                pool.sem_inc(sem(f"lo_ready{s}"), 1)
            with pool.Fori(0, DEPTH) as l:
                with pool.Fori(0, FFN_BLOCKS) as b:
                    low(0, base(l, 0, 0) + b)
                    low(1, base(l, 1, 0) + b)
                with pool.Fori(0, NW // 2) as b:
                    low(0, base(l, 0, 1) + b)
                    low(1, base(l, 1, 1) + b)
                low(0, base(l, 0, 1) + NW // 2)
                low(1, base(l, 1, 1) + NW // 2)
                low(0, base(l, 0, 1) + (NW + 1) // 2)
                for tt in range(TT):
                    q = l * TT + tt
                    nlev = SAMPLE_LEVELS if tt == PT else PROMPT_LEVELS
                    lev0 = levels_before(l, tt)
                    pool.wait_ge(sem("lt_ready"), q + 1)
                    for v in range(1, nlev):
                        if v >= 2:
                            pool.wait_ge(sem("t1_in1"), lev0 + v - 1)
                        nc.gpsimd.tensor_tensor(NT[:, v % 2], LTG[:, :, 0, :], LEV[:, v + 1, :].unsqueeze(1).broadcast_to([P, NH, P]), ALU.mult).then_inc(sem("blocks_ready"), 1)
                with pool.Fori(1, DC // 2) as b:
                    low(0, base(l, 0, 1) + (NW + 1) // 2 + b)
                    low(1, base(l, 1, 1) + NW // 2 + b)
                with pool.Fori(0, FFN_BLOCKS) as b:
                    low(0, base(l, 0, 2) + b)
                    low(1, base(l, 1, 2) + b)

        @block.scalar
        def _(act):
            A = nc.scalar.activation

            def round_weights(s, k):
                act.wait_ge(sem(f"raw_loaded{s}"), 16 * (k + 1))
                act.wait_ge(sem(f"block_used{s}"), k)
                A(WSP[s][:, 0], RAW[s][:], ACT.Copy).then_inc(sem(f"hi_ready{s}"), 1)

            def after_block(s, k):
                act.wait_ge(sem(f"block_used{s}"), k + 1)
                round_weights(s, k + 1)

            def prenorm(p):
                for c in range(DC):
                    act.wait_ge(sem("x_ready"), p * DC + c + 1)
                    if c >= 2:
                        act.wait_ge(sem("squares_summed"), p * DC + c - 1)
                    A(SQR[c % 2], XT[:, c, :], ACT.Square).then_inc(sem("squares"), 1)
                act.wait_ge(sem("squares_summed"), (p + 1) * DC)
                A(COLS[:], PS[:, 7, 0:TT], ACT.Sqrt, bias=EPSC[:, 0:1], scale=1.0 / D).then_inc(sem("pre_root"), 1)
                for c in range(DC):
                    act.wait_ge(sem("h_full"), p * DC + c + 1)
                    A(H[:, c, 0, :], SCR[:, c % 2, :], ACT.Copy).then_inc(sem("h_hi"), 1)

            def y_tiles(p, blocks, Y=Y):
                with act.Fori(0, DC // 2) as i:
                    for m in (0, 1):
                        blk = blocks(i, m)
                        for s, k in blk[:-1]:
                            after_block(s, k)
                        s, k = blk[-1]
                        after_block(s, k)
                        act.wait_ge(sem("y_copied"), 3 + p * DC + i * 2 + m)
                        act.wait_ge(sem("y_added"), 1 + p * DC + i * 2 + m)
                        A(SGB, Y[:, i * 2 + m, :], ACT.Square).then_inc(sem("y_squares"), 1)

            def postnorm(p, half):
                act.wait_ge(sem("post_summed"), p + 1)
                four = 4.0 if half else 1.0
                A(COLS[:], PS[:, 7, 0:TT], ACT.Sqrt, bias=EPSC[:, 1:2] if half else EPSC[:, 0:1], scale=four / D).then_inc(sem("post_root"), 1)

            def ffn(l, f):
                n = l * 2 + f
                with act.Fori(0, FT // 2) as i:
                    for jj in (0, 1):
                        j = i * 2 + jj
                        k0, k1 = base(l, 0, 2 * f) + j, base(l, 1, 2 * f) + j
                        act.wait_ge(sem("block_used0"), k0 + 1)
                        act.wait_ge(sem("hidden"), 2 + n * FT + j)
                        A(halves(SGB), pset(2 * jj), ACT.Silu).then_inc(sem("silu"), 1)
                        round_weights(0, k0 + 1)
                        after_block(1, k1)
                        act.wait_ge(sem("hidden"), 3 + n * FT + j)
                        A(HID[:, j, 0, :], HB, ACT.Copy).then_inc(sem("hidden_hi"), 1)
                y_tiles(l * 3 + 2 * f, lambda i, m: [((m * 3 + b) % 2, base(l, (m * 3 + b) % 2, 2 * f) + FT + i * 3 + (m * 3 + b) // 2) for b in range(3)])
                postnorm(l * 3 + 2 * f, True)

            act.wait_ge(sem("zeroed"), 1)
            nc.scalar.copy(EPSC[:, 2:3], EPSC[:, 0:1]).then_inc(sem("silu"), 1)
            act.drain()
            nc.scalar.copy(EPSC[:, 2:3], EPSC[:, 0:1]).then_inc(sem("y_squares"), 1)
            act.drain()
            nc.scalar.copy(EPSC[:, 2:3], EPSC[:, 0:1]).then_inc(sem("u_out"), 1)
            for name in ("silu", "u_out", "hi_ready0", "hi_ready1"):
                act.sem_inc(sem(name), 1)
            round_weights(0, 0)
            round_weights(1, 0)
            with act.Fori(0, DEPTH) as l:
                prenorm(l * 3)
                ffn(l, 0)
                prenorm(l * 3 + 1)
                for t, w in enumerate(W_TILES):
                    k = base(l, t % 2, 1) + t // 2
                    act.wait_ge(sem(f"block_used{t % 2}"), k + 1)
                    src = pset(t % 2)
                    if w in W_RWKV or w in W_POOL:
                        c, pre = (w - GC, 1) if w in W_RWKV else (w, POOL_ST)
                        dp, ds = (RWP, RWS) if w in W_RWKV else (PBP, PBS)
                        A(dp[:, c, pre:pre + HALF], src[:, 0, :], ACT.Copy)
                        A(dp[:, c, pre + HALF:pre + TP], src[:, 1, 0:TP - HALF], ACT.Copy)
                        A(ds[:, c, :, pre:], src[:, 1, TP - HALF:HALF].rearrange("p (b t) -> p b t", b=NSTR), ACT.Copy).then_inc(sem("u_out"), 1)
                    else:
                        dst = SBQ[:, w - W_SB[0], :] if w in W_SB else CV[:, w - W_CONV[0], :]
                        A(halves(dst), src, ACT.Copy).then_inc(sem("u_out"), 1)
                    round_weights(t % 2, k + 1)
                    if t == DECAY_AT - 1:
                        act.wait_ge(sem("ranks_shifted"), l + 1)
                        A(XS[0:32, 6, :], XS[0:32, 6, :], ACT.Tanh)
                        A(XS[64:128, 6, :], XS[64:128, 6, :], ACT.Sigmoid)
                        act.drain().then_inc(sem("gates_ready"), 1)
                    if t == DECAY_AT:
                        act.wait_ge(sem("decay_in"), l + 1)
                        for o in range(GC):
                            A(halves(CS[:, o, :]), pset(2 + o), ACT.Sigmoid, bias=vec("w0", o))
                        act.drain().then_inc(sem("decay_ready"), 1)
                    if t == A_AT:
                        act.wait_ge(sem("a_in"), l + 1)
                        for o in range(GC):
                            A(halves(BA[:, o, :]), pset(2 + o), ACT.Sigmoid, bias=vec("a0", o))
                        act.drain().then_inc(sem("a_ready"), 1)
                    if t == GATE_AT:
                        act.wait_ge(sem("gate_in"), l + 1)
                        for o in range(GC):
                            A(halves(GA[:, o, :]), pset(2 + o), ACT.Copy)
                        act.drain().then_inc(sem("gate_ready"), 1)
                    if t == KK_AT:
                        act.wait_ge(sem("kk_summed"), l + 1)
                        A(SCR[:].rearrange("p g (a n) -> p (g a) n", a=2), PS[:, 4:8, 0:HALF], ACT.Sqrt).then_inc(sem("kk_root"), 1)
                act.wait_ge(sem("conv_ready"), l + 1)
                A(H[:, 4:6, 0, :], CV[:, 4:6, :], ACT.Copy).then_inc(sem("conv_hi"), 1)
                act.wait_ge(sem("pool_out"), l + 1)
                for g in range(GC):
                    A(halves(H[:, g, 0, :]), pset(2 + g), ACT.Copy, scale=vec("pool_scale", g))
                act.drain().then_inc(sem("pool_hi"), 1)

                act.wait_ge(sem("attn_region"), l + 1)
                for i in range(TT):
                    act.wait_ge(sem("kv_turned"), l * TT + i + 1)
                    A(KT[:, i, :], PS[:, i % 2, 0:G], ACT.Copy)
                    A(VT[:, i, :], PS[:, i % 2, G:2 * G], ACT.Copy)
                    act.drain().then_inc(sem("kv_out"), 1)
                act.wait_ge(sem("kc_turned"), l + 1)
                A(KCT[:].rearrange("p g b n -> p (g b n)"), PSF[:, 1024:3072], ACT.Copy).then_inc(sem("kcT_out"), 1)

                def attnT_out(u):
                    act.wait_ge(sem("attn_turned"), l * UNITS + u + 1)
                    if u >= 2:
                        act.wait_ge(sem("attn_done"), l * UNITS + u - 1)
                    nb = (u // NH + 1) if u < PT * NH else 2
                    A(AT[:, u % 2, 0:nb, :], PS[:, 2 + u % 2, 0:nb * P].rearrange("p (b n) -> p b n", b=nb), ACT.Copy).then_inc(sem("attnT_out"), 1)

                for u in range(UNITS + 1):
                    if u < UNITS:
                        n = P * (u // NH + 1) if u < PT * NH else 2 * P
                        act.wait_ge(sem("z_ready"), l * UNITS + u + 1)
                        if u >= 2:
                            act.wait_ge(sem("attn_ready"), l * UNITS + u - 1)
                        A(KE[:, u % 2, 0:n], PS[:, u % 2, 0:n], ACT.Sigmoid, scale=-HD ** -0.5)
                        A(SIG[:, u % 2, 0:n], PS[:, u % 2, 0:n], ACT.Sigmoid, scale=HD ** -0.5)
                        act.drain().then_inc(sem("sig_ready"), 1)
                    if u >= 1:
                        attnT_out(u - 1)
                act.wait_ge(sem("attn_done"), (l + 1) * UNITS)
                A(H[:, 6:8, 0, 0:TP], PS[:, 4:6, :], ACT.Copy)
                A(H[:, 6:8, 0, TP:T], PS[:, 6:8, 0:P], ACT.Copy)
                act.drain().then_inc(sem("attn_hi"), 1)

                act.wait_ge(sem("rule_region"), l + 1)

                def exps(tt):
                    ts = slice(tt * P, (tt + 1) * P)
                    A(EXPS[:, 0], CS[:, :, ts], ACT.Exp, scale=-DECAY)
                    A(EXPS[:, 1], CS[:, :, ts], ACT.Exp, scale=DECAY)
                    A(EXPS[:, 2], CSP[:, :, ts], ACT.Exp, scale=-DECAY)
                    act.drain().then_inc(sem("exps_ready"), 1)

                exps(0)
                for tt in range(TT):
                    q = l * TT + tt
                    sample = tt == PT
                    ts = slice(tt * P, (tt + 1) * P)
                    act.wait_ge(sem("scores_in"), q + 1)
                    A(TOK[:, 0:2, :], PS[:, 5, :].rearrange("p (k n) -> p k n", k=2), ACT.Copy)
                    A(TOK[:, 2, :], PS[:, 6, 0:G], ACT.Copy)
                    act.drain().then_inc(sem("rows_ready"), 1)
                    if not sample:
                        exps(tt + 1)
                    for v in range(SAMPLE_LEVELS if sample else PROMPT_LEVELS):
                        for a in (0, 1):
                            act.wait_ge(sem(f"t1_in{a}"), levels_before(l, tt) + v + 1)
                            A(T1[:, 2 * a:2 * a + 2, :], PS[:, 4 + 2 * a, 0:256].rearrange("p (h n) -> p h n", h=2), ACT.Copy).then_inc(sem(f"t1_out{a}"), 1)
                    if not sample:
                        for c in range(NCH):
                            act.wait_ge(sem("u_in"), l * (PT * NCH + 1) + tt * NCH + c + 1)
                            A(NU[64 * c:64 * c + 64, :], PS[64 * c:64 * c + 64, 1, 0:G], ACT.Copy, scale=-1.0).then_inc(sem("u_done"), 1)
                    else:
                        act.wait_ge(sem("stateT_in"), l + 1)
                        A(STS[:].rearrange("p b g n -> p (b g n)"), PSF[:, 0:2048], ACT.Copy).then_inc(sem("stateT_out"), 1)
                        act.wait_ge(sem("state_rhs_in"), l + 1)
                        A(T1[:].rearrange("p h n -> p (h n)")[:, 0:G], PS[:, 4, 0:G], ACT.Copy).then_inc(sem("state_rhs_out"), 1)
                        act.wait_ge(sem("u_in"), l * (PT * NCH + 1) + PT * NCH + 1)
                        A(NU[:, :], PS[:, 1, 0:G], ACT.Copy, scale=-1.0).then_inc(sem("u_done"), 1)
                    act.wait_ge(sem("yr_in"), q + 1)
                    A(CSP[:, :, ts], PS[:, 2:4, 0:P], ACT.Copy).then_inc(sem("yr_out"), 1)
                    if tt == PT - 1:
                        act.wait_ge(sem("prompt_state_in"), l + 1)
                        A(ST[:], PS[:, 4, 0:G].rearrange("p (g n) -> p g n", g=2), ACT.Copy).then_inc(sem("prompt_state_out"), 1)
                    if sample:
                        act.wait_ge(sem("sample_state_in"), l + 1)
                        A(SBF[:, 0:2048], PSF[:, 0:2048], ACT.Copy).then_inc(sem("sample_state_out"), 1)
                act.wait_ge(sem("var_in"), l + 1)
                A(SCR[:].rearrange("p g (a n) -> p (g a) n", a=2), PS[:, 4:8, 0:HALF], ACT.Sqrt, bias=EPSC[:, 2:3], scale=1.0 / HD).then_inc(sem("var_root"), 1)
                act.wait_ge(sem("yr_ready"), l + 1)
                A(H[:, 2:4, 0, :], SCR[:], ACT.Copy).then_inc(sem("yr_hi"), 1)

                y_tiles(l * 3 + 1, lambda i, m: [(m, base(l, m, 1) + ((NW + 1) // 2, NW // 2)[m] + i)], YM)
                postnorm(l * 3 + 1, False)
                prenorm(l * 3 + 2)
                ffn(l, 1)
            for i in range(TT):
                act.wait_ge(sem("rows_in"), i + 1)
                A(IO[:, i, :], PSF[:, (i % 2) * 1024:(i % 2) * 1024 + 1024], ACT.Copy).then_inc(sem("out_rows"), 1)

        @block.vector
        def _(dve):
            V = nc.vector
            fence = dve.drain

            def prenorm(p):
                dve.wait_ge(sem("pre_root"), p + 1)
                rstd_rows()
                dve.wait_ge(sem("pre_spread"), p + 1)

                def full(c):
                    V.scalar_tensor_tensor(out=SCR[:, c % 2, :], in0=XT[:, c, :], scalar=vec("norm_g", norm_index + c),
                                           in1=PSF[:, 2048:2048 + T], op0=ALU.mult, op1=ALU.mult).then_inc(sem("h_full"), 1)

                full(0)
                for c in range(DC):
                    if c + 1 < DC:
                        full(c + 1)
                    fence()
                    dve.wait_ge(sem("h_hi"), p * DC + c + 1)
                    V.tensor_tensor(H[:, c, 1, :], SCR[:, c % 2, :], H[:, c, 0, :].bitcast(F32), ALU.subtract)
                    fence().then_inc(sem("h_ready"), 1)

            def rstd_rows():
                V.reciprocal(COLS[:], COLS[:])
                fence()
                V.tensor_tensor(ACC[:].rearrange("p (i n) -> p i n", i=TT), IDENT.unsqueeze(1).broadcast_to([P, TT, P]),
                                COLS[:].unsqueeze(2).broadcast_to([P, TT, P]), ALU.mult).then_inc(sem("diagonals"), 1)

            def y_tiles(p, blocks, Y=Y):
                V.memset(ACC[:], 0.0)
                fence()
                with dve.Fori(0, DC // 2) as i:
                    for m in (0, 1):
                        s, k = blocks(i, m)[-1]
                        dve.wait_ge(sem(f"block_used{s}"), k + 1)
                        V.tensor_copy(halves(Y[:, i * 2 + m, :]), pset(m)).then_inc(sem("y_copied"), 1)
                        dve.wait_ge(sem("y_squares"), 2 + p * DC + i * 2 + m)
                        V.tensor_tensor(ACC[:], ACC[:], SGB, ALU.add)
                        fence().then_inc(sem("y_added"), 1)

            def postnorm(p, Y=Y):
                dve.wait_ge(sem("post_root"), p + 1)
                rstd_rows()
                dve.wait_ge(sem("post_spread"), p + 1)
                for c in range(DC):
                    V.tensor_tensor(HB, Y[:, c, :], PSF[:, 2048:2048 + T], ALU.mult)
                    fence()
                    V.scalar_tensor_tensor(out=XT[:, c, :], in0=HB, scalar=vec("norm_g", norm_index + c), in1=XT[:, c, :],
                                           op0=ALU.mult, op1=ALU.add)
                    fence().then_inc(sem("x_ready"), 1)

            def ffn(l, f):
                n = l * 2 + f
                with dve.Fori(0, FT // 2) as i:
                    for jj in (0, 1):
                        j = i * 2 + jj
                        dve.wait_ge(sem("silu"), 3 + n * FT + j)
                        dve.wait_ge(sem("block_used1"), base(l, 1, 2 * f) + j + 1)
                        V.tensor_tensor(halves(HB), halves(SGB), pset(2 * jj + 1), ALU.mult)
                        fence().then_inc(sem("hidden"), 1)
                        dve.wait_ge(sem("hidden_hi"), n * FT + j + 1)
                        V.tensor_tensor(HID[:, j, 1, :], HB, HID[:, j, 0, :].bitcast(F32), ALU.subtract)
                        fence().then_inc(sem("hidden_split"), 1)

            V.memset(EPSC[:, 0:1], EPS)
            V.memset(EPSC[:, 1:2], 4 * EPS)
            V.memset(EPSC[:, 2:3], EPS)
            fence().then_inc(sem("zeroed"), 1)
            dve.wait_ge(sem("silu"), 2)
            dve.wait_ge(sem("y_squares"), 1)
            dve.wait_ge(sem("u_out"), 2)
            V.memset(EPSC[:, 2:3], GN_EPS)
            fence().then_inc(sem("hidden"), 1)
            fence().then_inc(sem("y_copied"), 1)
            for name in ("hidden", "y_copied", "y_added", "vec_ready"):
                dve.sem_inc(sem(name), 1)
            for i in range(TT):
                dve.wait_ge(sem("x_turned"), i + 1)
                V.tensor_copy(XT[:, :, i * P:(i + 1) * P], PSF[:, (i % 2) * 1024:(i % 2) * 1024 + 1024].rearrange("p (c n) -> p c n", c=DC))
                fence().then_inc(sem("x_placed"), 1)
            fence().then_inc(sem("x_ready"), DC)

            with dve.Fori(0, DEPTH) as l:
                dve.wait_ge(sem("vec_turned"), l + 1)
                V.tensor_copy(LV[:], PS[:, 6, 0:NV])
                fence()
                V.tensor_scalar(KA1[:], LV[:, VEC["k_a"][0]:VEC["k_a"][0] + GC], -1.0, 1.0, ALU.mult, ALU.add)
                fence().then_inc(sem("vec_ready"), 1)
                norm_index = 0
                prenorm(l * 3)
                ffn(l, 0)
                y_tiles(l * 3, lambda i, m: [((m * 3 + b) % 2, base(l, (m * 3 + b) % 2, 0) + FT + i * 3 + (m * 3 + b) // 2) for b in range(3)])
                norm_index = DC
                postnorm(l * 3)
                V.memset(RWP[:, :, 0:1], 0.0)
                V.memset(PBP[:, :, 0:POOL_ST], 0.0)
                V.memset(ZP[:, :, 0:2], 0.0)
                norm_index = 2 * DC
                prenorm(l * 3 + 1)
                V.memset(PW, 0.0)
                fence().then_inc(sem("poolw_zeroed"), 1)
                dve.wait_ge(sem("state_turned"), l + 1)
                ST7 = PS[:, 7, :]
                V.tensor_copy(RWS[:, :, :, 0], ST7[:, 0:RC * NSTR].rearrange("p (c b) -> p c b", c=RC))
                V.tensor_copy(ZS[:, :, :, 0:2], ST7[:, 64:96].rearrange("p (g b t) -> p g b t", g=GC, b=NSTR))
                V.tensor_copy(PBS[:, :, :, 0:POOL_ST], ST7[:, 128:368].rearrange("p (g b t) -> p g b t", g=GC, b=NSTR))
                fence().then_inc(sem("state_placed"), 1)
                for t in range(len(W_RWKV)):
                    c = W_RWKV[t] - GC
                    dve.wait_ge(sem("u_out"), 2 + l * NW + t + 1)
                    xp, xs = XS[:, c, 0:TP], XS[:, c, TP:T].rearrange("p (b t) -> p b t", b=NSTR)
                    V.tensor_tensor(xp, RWP[:, c, 0:TP], RWP[:, c, 1:1 + TP], ALU.subtract)
                    V.tensor_tensor(xs, RWS[:, c, :, 0:TS], RWS[:, c, :, 1:1 + TS], ALU.subtract)
                    fence()
                    V.scalar_tensor_tensor(out=xp, in0=xp, scalar=vec("mu", c), in1=RWP[:, c, 1:1 + TP], op0=ALU.mult, op1=ALU.add)
                    V.scalar_tensor_tensor(out=xs, in0=xs, scalar=vec("mu", c), in1=RWS[:, c, :, 1:1 + TS], op0=ALU.mult, op1=ALU.add)
                    if t == 0:
                        fence().then_inc(sem("ranks_shifted"), 1)
                    if t == 2:
                        fence()
                        for g in range(GC):
                            V.tensor_scalar(KK[:, g, :], XS[:, 2 + g, :], vec("k_k", g), None, ALU.mult)
                        fence()
                        V.tensor_tensor(SCR[:], KK[:], KK[:], ALU.mult)
                        fence().then_inc(sem("kk_squares"), 1)
                fence()
                R_, K_, V_ = XS[:, 0:2, :], XS[:, 2:4, :], XS[:, 4:6, :]
                dve.wait_ge(sem("tables_loaded"), (l + 1) * 3 * 16)
                dve.wait_ge(sem("decay_ready"), l + 1)
                for g in range(GC):
                    V.tensor_copy(CSP[:, g, :], CS[:, g, :])
                fence()
                for g in range(GC):
                    V.tensor_tensor_scan(CS[:, g, :], RESET[:], CSP[:, g, :], 0.0, ALU.mult, ALU.add)
                fence()
                V.tensor_tensor(CSP[:], CS[:], CSP[:], ALU.subtract)
                dve.wait_ge(sem("a_ready"), l + 1)
                for g in range(GC):
                    V.tensor_scalar(BV[:, g, :], BA[:, g, :], vec("k_a", g), KA1[:, g:g + 1], ALU.mult, ALU.add)
                fence()
                V.tensor_tensor(K_, K_, BV[:], ALU.mult)
                fence()
                for g in range(GC):
                    V.scalar_tensor_tensor(out=BV[:, g, :], in0=R_[:, g, :], scalar=vec("r_k", g), in1=K_[:, g, :], op0=ALU.mult, op1=ALU.mult)
                fence().then_inc(sem("bonus_in"), 1)
                dve.wait_ge(sem("kk_root"), l + 1)
                V.tensor_scalar(SCR[:], SCR[:], 1e-12, None, ALU.max)
                fence()
                V.reciprocal(SCR[:], SCR[:])
                fence()
                V.tensor_tensor(KK[:], KK[:], SCR[:], ALU.mult)
                fence()
                V.tensor_tensor(BA[:], BA[:], KK[:], ALU.mult)
                dve.wait_ge(sem("bonus_summed"), l + 1)
                V.tensor_tensor(BV[:].rearrange("p g (a n) -> p (g a) n", a=2), V_.rearrange("p g (a n) -> p (g a) n", a=2), PS[:, 4:8, 0:HALF], ALU.mult)
                fence()
                dve.wait_ge(sem("u_out"), 2 + l * NW + len(W_RWKV) + len(W_CONV))
                V.tensor_tensor(ZP[:, :, 2:], CV[:, 2:4, 0:TP], CV[:, 4:6, 0:TP], ALU.mult)
                for g in range(GC):
                    V.tensor_tensor(ZS[:, g, :, 2:], CV[:, 2 + g, TP:T].rearrange("p (b t) -> p b t", b=NSTR), CV[:, 4 + g, TP:T].rearrange("p (b t) -> p b t", b=NSTR), ALU.mult)
                fence()
                for g in range(GC):
                    yp, ys = CV[:, 2 + g, 0:TP], CV[:, 2 + g, TP:T].rearrange("p (b t) -> p b t", b=NSTR)
                    for w in range(CONV_W):
                        wv = vec("conv_w", w * GC + g)
                        zp, zs = ZP[:, g, w:w + TP], ZS[:, g, :, w:w + TS]
                        if w == 0:
                            V.tensor_scalar(yp, zp, wv, None, ALU.mult)
                            V.tensor_scalar(ys, zs, wv, None, ALU.mult)
                        else:
                            V.scalar_tensor_tensor(out=yp, in0=zp, scalar=wv, in1=yp, op0=ALU.mult, op1=ALU.add)
                            V.scalar_tensor_tensor(out=ys, in0=zs, scalar=wv, in1=ys, op0=ALU.mult, op1=ALU.add)
                        fence()
                V.tensor_tensor(CV[:, 4:6, :], CV[:, 2:4, :], CV[:, 0:2, :], ALU.mult)
                fence().then_inc(sem("conv_ready"), 1)
                dve.wait_ge(sem("u_out"), 2 + l * NW + len(W_RWKV) + len(W_CONV) + len(W_POOL))
                shift_t = TAIL[:, 0:63].rearrange("p (c n) -> p c n", c=RC)
                V.tensor_copy(shift_t[:, :, 0], RWP[:, :, TP])
                V.tensor_copy(shift_t[:, :, 1:9], RWS[:, :, :, TS])
                conv_t = TAIL[:, 64:100].rearrange("p (g n) -> p g n", g=GC)
                V.tensor_copy(conv_t[:, :, 0:2], ZP[:, :, TP:TP + 2])
                V.tensor_copy(conv_t[:, :, 2:18].rearrange("p g (b t) -> p g b t", b=NSTR), ZS[:, :, :, TS:TS + 2])
                V.tensor_copy(TAIL[:, 128:368].rearrange("p (g b t) -> p g b t", g=GC, b=NSTR), PBS[:, :, :, TS:TS + POOL_ST])
                V.tensor_copy(TAIL[:, 368:398].rearrange("p (g t) -> p g t", g=GC), PBP[:, :, TP:TP + POOL_ST])
                fence().then_inc(sem("tails_ready"), 1)
                NP, NSX = POOL_ST + TP, POOL_ST + TS
                DIF = CVF[:, 0:GC * T].rearrange("p (g t) -> p g t", g=GC)
                bufs = []
                for buf, at in ((CVF, GC * T), (OUTS, 1408 + G)):
                    bufs.append((buf[:, at:at + NP], buf[:, at + NP:at + NP + NSTR * NSX].rearrange("p (b t) -> p b t", b=NSTR)))
                for g in range(GC):
                    src = (PBP[:, g, :], PBS[:, g, :, :])
                    steps = ([(1, 0, 0), (2, 1, 64)] if g == 0 else [(1, 0, 0), (2, 1, 0), (4, 0, 0), (8, 1, 64)])
                    at = 0
                    for d, b, lo in steps:
                        at += d
                        V.tensor_tensor(bufs[b][0][lo:, at:], src[0][lo:, at:], src[0][lo:, at - d:NP - d], ALU.add)
                        V.tensor_tensor(bufs[b][1][lo:, :, at:], src[1][lo:, :, at:], src[1][lo:, :, at - d:NSX - d], ALU.add)
                        fence()
                        src = bufs[b]
                    for e in range(2):
                        pr = slice(64 * e, 64 * e + 64)
                        sp_, ss_ = bufs[e]
                        V.scalar_tensor_tensor(out=DIF[pr, g, 0:TP], in0=sp_[pr, POOL_ST:], scalar=IW[pr, g:g + 1], in1=PBP[pr, g, POOL_ST:], op0=ALU.mult, op1=ALU.subtract)
                        V.scalar_tensor_tensor(out=DIF[pr, g, TP:T].rearrange("p (b t) -> p b t", b=NSTR), in0=ss_[pr, :, POOL_ST:], scalar=IW[pr, g:g + 1], in1=PBS[pr, g, :, POOL_ST:], op0=ALU.mult, op1=ALU.subtract)
                    fence()
                    for e in range(2):
                        pr = slice(64 * e, 64 * e + 64)
                        V.tensor_tensor(DIF[pr, g, 0:16], bufs[e][0][pr, POOL_ST:POOL_ST + 16], ICNT[pr, g, :], ALU.mult)
                    fence()
                    V.tensor_tensor(DIF[:, g, 0:16], DIF[:, g, 0:16], PBP[:, g, POOL_ST:POOL_ST + 16], ALU.subtract)
                    fence()
                fence().then_inc(sem("pool_in"), 1)
                dve.wait_ge(sem("tails_turned"), l + 1)
                V.tensor_copy(OUTS[0:9, 0:RWKV_IN], PSF[0:9, 2048:2048 + RWKV_IN])
                V.tensor_copy(OUTS[0:18, 896:896 + G], PS[0:18, 6, 0:G])
                V.tensor_copy(OUTS[0:NSTR * POOL_ST, 1152:1152 + G], PS[0:NSTR * POOL_ST, 7, 0:G])
                V.tensor_copy(OUTS[0:POOL_ST, 1408:1408 + G], PS[0:POOL_ST, 7, G:2 * G])
                fence().then_inc(sem("tails_out"), 1)
                dve.wait_ge(sem("conv_hi"), l + 1)
                V.tensor_tensor(H[:, 4:6, 1, :], CV[:, 4:6, :], H[:, 4:6, 0, :].bitcast(F32), ALU.subtract)
                dve.wait_ge(sem("pool_hi"), l + 1)
                for g in range(GC):
                    V.scalar_tensor_tensor(out=halves(H[:, g, 1, :]), in0=pset(2 + g), scalar=vec("pool_scale", g), in1=halves(H[:, g, 0, :].bitcast(F32)), op0=ALU.mult, op1=ALU.subtract)
                fence()
                dve.wait_ge(sem("tails_stored"), (l + 1) * 6 * 16)
                V.memset(QM[:], 0.0)
                fence().then_inc(sem("attn_region"), 1)
                for g in range(GC):
                    V.tensor_copy(QM[:, g, :].rearrange("p (b n) -> p b n", b=NSTR)[:, :, 0:TS], SBQ[:, g, TP:T].rearrange("p (b t) -> p b t", b=NSTR))
                fence().then_inc(sem("qm_ready"), 1)
                for u in range(UNITS):
                    n = P * (u // NH + 1) if u < PT * NH else 2 * P
                    s = u % 2
                    dve.wait_ge(sem("sig_ready"), l * UNITS + u + 1)
                    ke = KE[:, s, :]
                    V.memset(ke[:, n:n + 1], 1.0)
                    V.tensor_tensor_scan(ke[:, n - 1::-1], ke[:, n - 1::-1], ke[:, n - 1::-1], 1.0, ALU.mult, ALU.bypass)
                    fence()
                    if u >= 2:
                        dve.wait_ge(sem("attn_turned"), l * UNITS + u - 1)
                    V.tensor_tensor(AW[:, s, 0:n], SIG[:, s, 0:n], ke[:, 1:n + 1], ALU.mult)
                    fence().then_inc(sem("attn_ready"), 1)
                dve.wait_ge(sem("attn_hi"), l + 1)
                V.tensor_tensor(H[:, 6:8, 1, 0:TP], PS[:, 4:6, :], H[:, 6:8, 0, 0:TP].bitcast(F32), ALU.subtract)
                V.tensor_tensor(H[:, 6:8, 1, TP:T], PS[:, 6:8, 0:P], H[:, 6:8, 0, TP:T].bitcast(F32), ALU.subtract)
                fence()
                dve.wait_ge(sem("kv_stored"), (l + 1) * 4 * 16)
                V.memset(SN.rearrange("p b g n -> p (b g n)"), 0.0)
                V.memset(AR[:], 0.0)
                V.memset(ST[:], 0.0)
                V.memset(RH[:], 0.0)
                V.memset(NU[:], 0.0)
                fence().then_inc(sem("rule_region"), 1)
                dve.wait_ge(sem("masks_loaded"), (l + 1) * 4 * 16)

                def operands(tt):
                    ts = slice(tt * P, (tt + 1) * P)
                    dve.wait_ge(sem("exps_ready"), l * TT + tt + 1)
                    EP, EN, EPP = EXPS[:, 0], EXPS[:, 1], EXPS[:, 2]
                    per = TS if tt == PT else CH
                    n = P // per
                    AF, RF, PC = AFS[:, tt % 2], RFS[:, tt % 2], PCS[:, tt % 2]
                    V.tensor_tensor(BK[:, 0], EN, BA[:, :, ts], ALU.mult)
                    V.tensor_tensor(BK[:, 1], EN, K_[:, :, ts], ALU.mult)
                    V.tensor_tensor(AF, EPP, KK[:, :, ts], ALU.mult)
                    V.tensor_tensor(RF, EP, R_[:, :, ts], ALU.mult)
                    V.tensor_copy(PC[:, :, 0:n], EP.rearrange("p g (c n) -> p g c n", n=per)[:, :, :, per - 1])
                    fence()
                    for e in range(2):
                        pr = slice(64 * e, 64 * e + 64)
                        V.tensor_copy(AR[pr, e, :, 0, :], AF[pr])
                        V.tensor_copy(AR[pr, e, :, 1, :], RF[pr])
                    for k in range(2):
                        V.tensor_tensor(BP[:, k].rearrange("p g (c n) -> p g c n", n=per), BK[:, k].rearrange("p g (c n) -> p g c n", n=per),
                                        PC[:, :, 0:n].unsqueeze(3).broadcast_to([P, GC, n, per]), ALU.mult)
                    fence().then_inc(sem("operands"), 1)

                operands(0)
                for tt in range(TT):
                    q = l * TT + tt
                    sample = tt == PT
                    ts = slice(tt * P, (tt + 1) * P)
                    AF, RF, PC = AFS[:, tt % 2], RFS[:, tt % 2], PCS[:, tt % 2]
                    nlev = SAMPLE_LEVELS if sample else PROMPT_LEVELS
                    lev0, inner0 = levels_before(l, tt), inner_levels_before(l, tt)
                    dve.wait_ge(sem("scores_in"), q + 1)
                    if sample:
                        dve.wait_ge(sem("sample_tri_loaded"), (l + 1) * 16)
                    tri = TRI[:].rearrange("p a n -> p (a n)").unsqueeze(1).broadcast_to([P, NH, 2 * P])

                    def by_head(ap):
                        return ap.rearrange("p (h n) -> p h n", n=P)

                    def every_head(ap, n=NH):
                        return ap.unsqueeze(1).broadcast_to([P, n, P])

                    V.tensor_tensor(LTG[:].rearrange("p h a n -> p h (a n)"), PSF[:, 0:1024].rearrange("p (h n) -> p h n", h=NH), tri, ALU.mult)
                    V.tensor_tensor(X[:], by_head(PS[:, 4, :]), every_head(LEV1[:]), ALU.mult)
                    fence().then_inc(sem("lt_ready"), 1)
                    V.tensor_tensor(NT[:, 0], LTG[:, :, 0, :], every_head(LEV[:, 1, :]), ALU.mult)
                    V.tensor_tensor(XTR[:], LTG[:, :, 0, :], every_head(LEV[:, 0, :]), ALU.mult)
                    fence()
                    for a in (0, 1):
                        hs = slice(2 * a, 2 * a + 2)
                        V.tensor_tensor(X[:, hs], every_head(IDENT, 2), X[:, hs], ALU.subtract).then_inc(sem(f"x_ready{a}"), 1)
                    for a in (0, 1):
                        hs = slice(2 * a, 2 * a + 2)
                        V.tensor_tensor(XTR[:, hs], every_head(IDENT, 2), XTR[:, hs], ALU.subtract).then_inc(sem(f"xt_ready{a}"), 1)
                    dve.wait_ge(sem("kappa_scores_in"), q + 1)
                    V.tensor_tensor(KTG[:].rearrange("p h a n -> p h (a n)"), PSF[:, 1024:2048].rearrange("p (h n) -> p h n", h=NH), tri, ALU.mult)
                    fence().then_inc(sem("scores_masked"), 1)
                    for v in range(nlev):
                        for a in (0, 1):
                            hs = slice(2 * a, 2 * a + 2)
                            if v + 1 < nlev:
                                dve.wait_ge(sem(f"x_update_in{a}"), inner0 + v + 1)
                                V.tensor_tensor(X[:, hs], X[:, hs], by_head(PS[:, 4 + 2 * a, 256:512]), ALU.subtract).then_inc(sem(f"x_ready{a}"), 1)
                            dve.wait_ge(sem(f"xt_update_in{a}"), lev0 + v + 1)
                            V.tensor_tensor(XTR[:, hs], XTR[:, hs], by_head(PS[:, 5 + 2 * a, 0:256]), ALU.subtract).then_inc(sem(f"xt_ready{a}"), 1)
                        if v == 0:
                            dve.wait_ge(sem("mv_in"), q + 1)
                            V.tensor_copy(MVS[:], PS[:, 0, G:2 * G])
                        if v == 1 and not sample:
                            operands(tt + 1)
                    fence()
                    if not sample:
                        for c in range(NCH):
                            r = slice(64 * c, 64 * c + 64)
                            dve.wait_ge(sem("rhs_in"), l * (PT * NCH + 1) + tt * NCH + c + 1)
                            V.tensor_tensor(RH[r, :], PS[r, 0, 0:G], MVS[r, :], ALU.add).then_inc(sem("rhs_ready"), 1)
                            dve.wait_ge(sem("state_in"), l * PT * NCH + tt * NCH + c + 1)
                            for g in range(GC):
                                for e in range(2):
                                    pr = slice(64 * e, 64 * e + 64)
                                    V.scalar_tensor_tensor(out=ST[pr, g, pr], in0=ST[pr, g, pr], scalar=PC[pr, g, c:c + 1],
                                                           in1=PS[pr, 4, g * P + 64 * e:g * P + 64 * e + 64], op0=ALU.mult, op1=ALU.add)
                            fence().then_inc(sem("state_ready"), 1)
                    else:
                        dve.wait_ge(sem("rhs_in"), l * (PT * NCH + 1) + PT * NCH + 1)
                        V.tensor_tensor(RH[:], PS[:, 0, 0:G], MVS[:], ALU.add).then_inc(sem("rhs_ready"), 1)
                        dve.wait_ge(sem("u_done"), l * (PT * NCH + 1) + PT * NCH + 1)
                        for h in range(NH):
                            g, e = h // 2, h % 2
                            pr = slice(64 * e, 64 * e + 64)
                            if h:
                                dve.wait_ge(sem("sample_delta"), l * NH + h)
                            rows = ROWM[:].unsqueeze(2).broadcast_to([P, NSTR, HD])
                            V.tensor_tensor(NM[:, 0], NU[:, h * HD:(h + 1) * HD].unsqueeze(1).broadcast_to([P, NSTR, HD]), rows, ALU.mult)
                            V.tensor_tensor(NM[:, 1], TOK[:, 2, h * HD:(h + 1) * HD].unsqueeze(1).broadcast_to([P, NSTR, HD]), rows, ALU.mult)
                            fence().then_inc(sem("spread_u"), 1)
                            dve.wait_ge(sem("sample_delta"), l * NH + h + 1)
                            sv = STS[pr, :, g, pr]
                            pc = PC[pr, g, :].unsqueeze(2).broadcast_to([64, NSTR, HD])
                            V.tensor_tensor(sv, sv, pc, ALU.mult)
                            fence()
                            V.tensor_tensor(sv, sv, PS[pr, 4 + h, :].rearrange("p (b n) -> p b n", b=NSTR), ALU.add)
                            fence()
                        fence().then_inc(sem("sample_states"), 1)
                    fence()
                dve.wait_ge(sem("mean_in"), l + 1)
                flat = lambda a: a.rearrange("p g (a n) -> p (g a) n", a=2)
                V.scalar_tensor_tensor(out=flat(CSP[:]), in0=PS[:, 0:4, 0:HALF], scalar=-1.0 / HD, in1=flat(CSP[:]), op0=ALU.mult, op1=ALU.add)
                fence()
                V.tensor_tensor(SCR[:], CSP[:], CSP[:], ALU.mult)
                fence().then_inc(sem("centred"), 1)
                dve.wait_ge(sem("var_root"), l + 1)
                V.reciprocal(SCR[:], SCR[:])
                fence()
                V.tensor_tensor(SCR[:], SCR[:], CSP[:], ALU.mult)
                fence()
                for g in range(GC):
                    V.tensor_scalar(SCR[:, g, :], SCR[:, g, :], vec("ln_w", g), vec("ln_b", g), ALU.mult, ALU.add)
                fence()
                V.tensor_tensor(SCR[:], SCR[:], BV[:], ALU.add)
                fence()
                V.tensor_tensor(SCR[:], SCR[:], GA[:], ALU.mult)
                fence().then_inc(sem("yr_ready"), 1)
                dve.wait_ge(sem("yr_hi"), l + 1)
                V.tensor_tensor(H[:, 2:4, 1, :], SCR[:], H[:, 2:4, 0, :].bitcast(F32), ALU.subtract)
                fence().then_inc(sem("mixed"), 1)
                dve.wait_ge(sem("wkv_stored"), (l + 1) * 8 * 16)
                y_tiles(l * 3 + 1, lambda i, m: [(m, base(l, m, 1) + ((NW + 1) // 2, NW // 2)[m] + i)], YM)
                norm_index = 3 * DC
                postnorm(l * 3 + 1, YM)
                norm_index = 4 * DC
                prenorm(l * 3 + 2)
                ffn(l, 1)
                y_tiles(l * 3 + 2, lambda i, m: [((m * 3 + b) % 2, base(l, (m * 3 + b) % 2, 2) + FT + i * 3 + (m * 3 + b) // 2) for b in range(3)])
                norm_index = 5 * DC
                postnorm(l * 3 + 2)

        @block.tensor
        def _(pe):
            MM = nc.tensor.matmul

            def turn(out, in_):
                return nc.tensor.transpose(out, in_, IDENT[0:in_.shape[0], 0:in_.shape[0]])

            def split_product(q, s, slot, mov, first, last):
                hi, lo = WSP[s][:, 0, slot, :], WSP[s][:, 1, slot, :]
                for a in (0, 1):
                    out = PS[:, 2 * q + a, 0:HALF]
                    cols = slice(a * HALF, (a + 1) * HALF)
                    MM(out, hi, mov[:, 0, cols], start=first, stop=False)
                    MM(out, hi, mov[:, 1, cols], start=False, stop=False)
                    end = MM(out, lo, mov[:, 0, cols], start=False, stop=last)
                return end

            def token_sums(src, first, last):
                for i in range(TT):
                    end = MM(PS[:, 7, i:i + 1], src[:, i * P:(i + 1) * P], ONES[:, 0:1], start=first and i == 0, stop=last, skip_group_check=True)
                return end

            def spread():
                MM(PS[:, 4, :], ONES, ACC[:, 0:512], start=True, stop=True)
                return MM(PS[:, 5, 0:P], ONES, ACC[:, 512:T], start=True, stop=True)

            def prenorm(p):
                for c in range(DC):
                    pe.wait_ge(sem("squares"), p * DC + c + 1)
                    token_sums(SQR[c % 2], c == 0, c == DC - 1).then_inc(sem("squares_summed"), 1)
                pe.wait_ge(sem("diagonals"), 2 * p + 1)
                spread().then_inc(sem("pre_spread"), 1)

            def postnorm(p):
                pe.wait_ge(sem("y_added"), 1 + (p + 1) * DC)
                token_sums(ACC[:], True, True).then_inc(sem("post_summed"), 1)
                pe.wait_ge(sem("diagonals"), 2 * p + 2)
                spread().then_inc(sem("post_spread"), 1)

            def from_h(q, s, k, p, wait_h):
                pe.wait_ge(sem(f"lo_ready{s}"), k + 2)
                for c in range(DC):
                    if wait_h:
                        pe.wait_ge(sem("h_ready"), p * DC + c + 1)
                    end = split_product(q, s, c, H[:, c], c == 0, c == DC - 1)
                end.then_inc(sem(f"block_used{s}"), 1)

            def ffn(l, f):
                n, p = l * 2 + f, l * 3 + 2 * f
                with pe.Fori(0, FT // 2) as i:
                    for jj in (0, 1):
                        j = i * 2 + jj
                        pe.wait_ge(sem("silu"), 1 + n * FT + j)
                        from_h(2 * jj, 0, base(l, 0, 2 * f) + j, p, jj == 0)
                        pe.wait_ge(sem("hidden"), 1 + n * FT + j)
                        from_h(2 * jj + 1, 1, base(l, 1, 2 * f) + j, p, False)
                with pe.Fori(0, DC // 2) as i:
                    for m in (0, 1):
                        pe.wait_ge(sem("y_copied"), 1 + p * DC + i * 2 + m)
                        pe.wait_ge(sem("hidden"), 1 + n * FT + FT)
                        for b, (r0, r1) in enumerate(DOWN_CUTS):
                            s = (m * 3 + b) % 2
                            pe.wait_ge(sem(f"lo_ready{s}"), base(l, s, 2 * f) + FT + i * 3 + (m * 3 + b) // 2 + 2)
                            if m == 0:
                                pe.wait_ge(sem("hidden_split"), n * FT + r1)
                            for r in range(r0, r1):
                                end = split_product(m, s, r - r0, HID[:, r], r == 0, r == FT - 1)
                            end.then_inc(sem(f"block_used{s}"), 1)
                postnorm(p)

            pe.wait_ge(sem("consts_loaded"), 16)
            for i in range(TT):
                pe.wait_ge(sem(f"x_loaded{i}"), 16)
                if i >= 2:
                    pe.wait_ge(sem("x_placed"), i - 1)
                for c in range(DC):
                    at = (i % 2) * 1024 + c * P
                    end = turn(PSF[:, at:at + P], IO[:, i, c * P:(c + 1) * P])
                end.then_inc(sem("x_turned"), 1)
            with pe.Fori(0, DEPTH) as l:
                pe.wait_ge(sem("vec_loaded"), (l + 1) * len(VEC) * 16)
                turn(PS[:, 6, 0:NV], VROW[:]).then_inc(sem("vec_turned"), 1)
                prenorm(l * 3)
                ffn(l, 0)
                prenorm(l * 3 + 1)
                def rank_product(lo, hi):
                    for o in range(GC):
                        for a in (0, 1):
                            end = MM(PS[:, 2 * (2 + o) + a, 0:HALF], SMALLW[lo:hi, o * P:(o + 1) * P], XS[lo:hi, 6, a * HALF:(a + 1) * HALF], start=True, stop=True)
                    return end

                def head_sums(src, q):
                    for g in range(GC):
                        for a in (0, 1):
                            end = MM(PS[:, 2 * (q + g) + a, 0:HALF], HEADS, src[:, g, a * HALF:(a + 1) * HALF], start=True, stop=True)
                    return end

                for t in range(NW):
                    pe.wait_ge(sem("u_out"), 1 + l * NW + t)
                    from_h(t % 2, t % 2, base(l, t % 2, 1) + t // 2, l * 3 + 1, t == 0)
                    if t == STATES_AT:
                        pe.wait_ge(sem("state_loaded"), (l + 1) * 3 * 16)
                        for g in range(GC):
                            turn(PS[:, 7, 128 + 120 * g:248 + 120 * g], STIN2[0:120, G + g * P:G + (g + 1) * P])
                        for g in range(GC):
                            turn(PS[:, 7, 64 + 16 * g:80 + 16 * g], STIN2[0:16, g * P:(g + 1) * P])
                        for c in range(RC):
                            end = turn(PS[:, 7, c * NSTR:(c + 1) * NSTR], STIN[0:NSTR, c * P:(c + 1) * P])
                        end.then_inc(sem("state_turned"), 1)
                    if t == DECAY_AT:
                        pe.wait_ge(sem("rank_loaded"), (l + 1) * 3 * 16)
                        pe.wait_ge(sem("gates_ready"), l + 1)
                        pe.wait_ge(sem("state_placed"), l + 1)
                        rank_product(0, 32).then_inc(sem("decay_in"), 1)
                    if t == A_AT:
                        pe.wait_ge(sem("decay_ready"), l + 1)
                        rank_product(32, 64).then_inc(sem("a_in"), 1)
                    if t == GATE_AT:
                        pe.wait_ge(sem("a_ready"), l + 1)
                        rank_product(64, 128).then_inc(sem("gate_in"), 1)
                    if t == KK_AT:
                        pe.wait_ge(sem("kk_squares"), l + 1)
                        pe.wait_ge(sem("gate_ready"), l + 1)
                        head_sums(SCR, 2).then_inc(sem("kk_summed"), 1)
                    if t == BONUS_AT:
                        pe.wait_ge(sem("kk_root"), l + 1)
                        pe.wait_ge(sem("bonus_in"), l + 1)
                        head_sums(BV, 2).then_inc(sem("bonus_summed"), 1)
                    if t == TAILS_AT:
                        pe.wait_ge(sem("tails_ready"), l + 1)
                        for c in range(RC):
                            turn(PSF[0:9, 2048 + c * P:2048 + (c + 1) * P], TAIL[:, c * 9:(c + 1) * 9])
                        for g in range(GC):
                            turn(PS[0:18, 6, g * P:(g + 1) * P], TAIL[:, 64 + 18 * g:82 + 18 * g])
                        for g in range(GC):
                            turn(PS[0:120, 7, g * P:(g + 1) * P], TAIL[:, 128 + 120 * g:248 + 120 * g])
                        for g in range(GC):
                            end = turn(PS[0:15, 7, G + g * P:G + (g + 1) * P], TAIL[:, 368 + 15 * g:383 + 15 * g])
                        end.then_inc(sem("tails_turned"), 1)
                pe.wait_ge(sem("poolw_loaded"), (l + 1) * 4 * 16)
                pe.wait_ge(sem("tails_out"), l + 1)
                pe.wait_ge(sem("pool_in"), l + 1)
                for g in range(GC):
                    for a in (0, 1):
                        end = MM(PS[:, 2 * (2 + g) + a, 0:HALF], PW[:, g, :], CVF[:, g * T + a * HALF:g * T + (a + 1) * HALF], start=True, stop=True)
                end.then_inc(sem("pool_out"), 1)

                pe.wait_ge(sem("attn_region"), l + 1)
                for i in range(TT):
                    if i >= 2:
                        pe.wait_ge(sem("kv_out"), l * TT + i - 1)
                    for c in range(4):
                        end = turn(PS[:, i % 2, c * P:(c + 1) * P], SBQ[:, 2 + c, i * P:(i + 1) * P])
                    end.then_inc(sem("kv_turned"), 1)
                pe.wait_ge(sem("kc_loaded"), (l + 1) * 16)
                for g in range(GC):
                    for b in range(NSTR):
                        at = 1024 + (g * NSTR + b) * P
                        end = turn(PSF[:, at:at + P], KC[:, b, g * P:(g + 1) * P])
                end.then_inc(sem("kc_turned"), 1)

                def scores(u):
                    i, h = u // NH, u % NH
                    pr, g = slice(64 * (h % 2), 64 * (h % 2) + 64), h // 2
                    if u >= 2:
                        pe.wait_ge(sem("sig_ready"), l * UNITS + u - 1)
                    z = PS[:, u % 2, :]
                    if i < PT:
                        n = (i + 1) * P
                        MM(z[:, n - P:n], IDENT, SEE[0], start=True, stop=False, skip_group_check=True)
                        end = MM(z[:, 0:n], SBQ[pr, g, i * P:(i + 1) * P], SBQ[pr, 2 + g, 0:n], start=False, stop=True, skip_group_check=True)
                    else:
                        n = 2 * P
                        MM(z[:, PAST:n], IDENT, SEE[1], start=True, stop=False, skip_group_check=True)
                        MM(z[:, PAST:n], SBQ[pr, g, TP:T], SBQ[pr, 2 + g, TP:T], start=False, stop=True, skip_group_check=True)
                        for b in range(NSTR):
                            end = MM(z[:, 0:PAST], QM[pr, g, b * P:(b + 1) * P], KCT[pr, g, b, :], start=False, stop=b == NSTR - 1, skip_group_check=True)
                    end.then_inc(sem("z_ready"), 1)

                def turn_attn(u):
                    nb = (u // NH + 1) if u < PT * NH else 2
                    pe.wait_ge(sem("attn_ready"), l * UNITS + u + 1)
                    if u >= 2:
                        pe.wait_ge(sem("attnT_out"), l * UNITS + u - 1)
                    for b in range(nb):
                        end = turn(PS[:, 2 + u % 2, b * P:(b + 1) * P], AW[:, u % 2, b * P:(b + 1) * P])
                    end.then_inc(sem("attn_turned"), 1)

                def values(u):
                    i, h = u // NH, u % NH
                    pr, g = slice(64 * (h % 2), 64 * (h % 2) + 64), h // 2
                    hc = slice(h * HD, (h + 1) * HD)
                    pe.wait_ge(sem("attnT_out"), l * UNITS + u + 1)
                    if i < PT:
                        for b in range(i + 1):
                            end = MM(PS[pr, 4 + g, i * P:(i + 1) * P], VT[:, b, hc], AT[:, u % 2, b, :], start=b == 0, stop=b == i)
                    else:
                        MM(PS[pr, 6 + g, 0:P], VT[:, PT, hc], AT[:, u % 2, 1, :], start=True, stop=False, skip_group_check=True)
                        for b in range(NSTR):
                            end = MM(PS[pr, 6 + g, b * TS:(b + 1) * TS], VC[:, b, hc], AT[:, u % 2, 0, b * TS:(b + 1) * TS], start=False, stop=b == NSTR - 1, skip_group_check=True)
                    end.then_inc(sem("attn_done"), 1)

                pe.wait_ge(sem("kcT_out"), l + 1)
                pe.wait_ge(sem("kv_out"), (l + 1) * TT)
                pe.wait_ge(sem("pool_hi"), l + 1)
                pe.wait_ge(sem("qm_ready"), l + 1)
                pe.wait_ge(sem("vc_loaded"), (l + 1) * 16)
                for u in range(UNITS + 2):
                    if u < UNITS:
                        scores(u)
                    if 1 <= u <= UNITS:
                        turn_attn(u - 1)
                    if u >= 2:
                        values(u - 2)

                pe.wait_ge(sem("rule_region"), l + 1)
                pe.wait_ge(sem("attn_hi"), l + 1)

                def heads():
                    for h in range(NH):
                        yield h, h // 2, h % 2, slice(h * HD, (h + 1) * HD), slice(64 * (h % 2), 64 * (h % 2) + 64)

                for tt in range(TT):
                    q = l * TT + tt
                    sample = tt == PT
                    ts = slice(tt * P, (tt + 1) * P)
                    nlev = SAMPLE_LEVELS if sample else PROMPT_LEVELS
                    lev0, inner0 = levels_before(l, tt), inner_levels_before(l, tt)
                    AF, RF = AFS[:, tt % 2], RFS[:, tt % 2]
                    pe.wait_ge(sem("operands"), q + 1)
                    for k in range(2):
                        for g in range(GC):
                            turn(PS[:, 5, (2 * k + g) * P:(2 * k + g + 1) * P], BP[:, k, g, :])
                    for g in range(GC):
                        turn(PS[:, 6, g * P:(g + 1) * P], XS[:, 4 + g, ts])
                    for h, g, e, hc, pr in heads():
                        MM(PSF[:, h * 256:h * 256 + 256], BK[:, 0, g, :], AR[:, e, g, :, :].rearrange("p a n -> p (a n)"), start=True, stop=True)
                    if sample:
                        pe.wait_ge(sem("prompt_state_out"), l + 1)
                    elif tt:
                        pe.wait_ge(sem("state_ready"), l * PT * NCH + tt * NCH)
                    for h, g, e, hc, pr in heads():
                        end = MM(PS[:, 4, h * P:(h + 1) * P], AR[:, e, g, 0, :], BK[:, 0, g, :], start=True, stop=True)
                    end.then_inc(sem("scores_in"), 1)
                    if tt:
                        pe.wait_ge(sem("yr_out"), q)
                    for h, g, e, hc, pr in heads():
                        end = MM(PSF[:, 1024 + h * 256:1280 + h * 256], BK[:, 1, g, :], AR[:, e, g, :, :].rearrange("p a n -> p (a n)"), start=True, stop=True)
                    end.then_inc(sem("kappa_scores_in"), 1)
                    pe.wait_ge(sem("rows_ready"), q + 1)
                    for v in range(nlev):
                        if v:
                            pe.wait_ge(sem("blocks_ready"), inner0 + v)
                        for a in (0, 1):
                            pe.wait_ge(sem(f"x_ready{a}"), lev0 + v + 1)
                            for h in (2 * a, 2 * a + 1):
                                end = MM(PS[:, 4 + 2 * a, (h % 2) * P:(h % 2 + 1) * P], NT[:, v % 2, h, :], X[:, h, :], start=True, stop=True)
                            end.then_inc(sem(f"t1_in{a}"), 1)
                        if v == 0:
                            pe.wait_ge(sem("scores_masked"), q + 1)
                            for h, g, e, hc, pr in heads():
                                end = MM(PS[:, 0, G + h * HD:G + (h + 1) * HD], KTG[:, h, 0, :], TOK[:, 2, hc], start=True, stop=True)
                            end.then_inc(sem("mv_in"), 1)
                            if not sample:
                                for h, g, e, hc, pr in heads():
                                    MM(PS[pr, 2 + g, 0:P], TOK[:, 2, hc], KTG[:, h, 1, :], start=True, stop=False, skip_group_check=True)
                        for a in (0, 1):
                            pe.wait_ge(sem(f"t1_out{a}"), lev0 + v + 1)
                            pe.wait_ge(sem(f"xt_ready{a}"), lev0 + q + v + 1)
                            if v + 1 < nlev:
                                for h in (2 * a, 2 * a + 1):
                                    end = MM(PS[:, 4 + 2 * a, 256 + (h % 2) * P:256 + (h % 2 + 1) * P], XTR[:, h, :], T1[:, h, :], start=True, stop=True)
                                end.then_inc(sem(f"x_update_in{a}"), 1)
                            for h in (2 * a, 2 * a + 1):
                                end = MM(PS[:, 5 + 2 * a, (h % 2) * P:(h % 2 + 1) * P], T1[:, h, :], XTR[:, h, :], start=True, stop=True)
                            end.then_inc(sem(f"xt_update_in{a}"), 1)
                    for a in (0, 1):
                        pe.wait_ge(sem(f"xt_ready{a}"), lev0 + q + nlev + 1)
                    if not sample:
                        for c in range(NCH):
                            r, n = slice(64 * c, 64 * c + 64), tt * NCH + c
                            if n:
                                pe.wait_ge(sem("state_ready"), l * PT * NCH + n)
                            for g in range(GC):
                                end = MM(PS[r, 0, g * P:(g + 1) * P], AF[:, g, r], ST[:, g, :], start=True, stop=True)
                            end.then_inc(sem("rhs_in"), 1)
                            for g in range(GC):
                                MM(PS[:, 2 + g, r], ST[:, g, :], RF[:, g, r], start=False, stop=False, skip_group_check=True)
                            for g in range(GC):
                                gc = slice(g * P, (g + 1) * P)
                                MM(PS[:, 4, gc], TOK[r, 1, gc], TOK[r, 2, gc], start=g == 0, stop=False, skip_group_check=True)
                            pe.wait_ge(sem("rhs_ready"), l * (PT * NCH + 1) + n + 1)
                            for h, g, e, hc, pr in heads():
                                end = MM(PS[r, 1, hc], XTR[:, h, r], RH[:, hc], start=True, stop=True)
                            end.then_inc(sem("u_in"), 1)
                            pe.wait_ge(sem("u_done"), l * (PT * NCH + 1) + n + 1)
                            for g in range(GC):
                                gc = slice(g * P, (g + 1) * P)
                                end = MM(PS[:, 4, gc], TOK[r, 0, gc], NU[r, gc], start=False, stop=True, skip_group_check=True)
                            end.then_inc(sem("state_in"), 1)
                            for h, g, e, hc, pr in heads():
                                end = MM(PS[pr, 2 + g, r], NU[:, hc], LTG[:, h, 1, r], start=False, stop=True, skip_group_check=True)
                        end.then_inc(sem("yr_in"), 1)
                        if tt == PT - 1:
                            pe.wait_ge(sem("state_ready"), (l + 1) * PT * NCH)
                            for g in range(GC):
                                end = turn(PS[:, 4, g * P:(g + 1) * P], ST[:, g, :])
                            end.then_inc(sem("prompt_state_in"), 1)
                    else:
                        pe.wait_ge(sem("wkv_loaded"), (l + 1) * 4 * 16)
                        for b in range(NSTR):
                            for g in range(GC):
                                at = (b * GC + g) * P
                                end = turn(PSF[:, at:at + P], SN[:, b, g, :])
                        end.then_inc(sem("stateT_in"), 1)
                        pe.wait_ge(sem("stateT_out"), l + 1)
                        for h, g, e, hc, pr in heads():
                            MM(PS[pr, 2 + g, 0:P], TOK[:, 2, hc], KTG[:, h, 1, :], start=True, stop=False, skip_group_check=True)
                        for b in range(NSTR):
                            for g in range(GC):
                                cs = slice(g * P + b * TS, g * P + (b + 1) * TS)
                                end = MM(PS[:, 4, cs], STS[:, b, g, :], AF[:, g, b * TS:(b + 1) * TS], start=True, stop=True)
                        end.then_inc(sem("state_rhs_in"), 1)
                        for b in range(NSTR):
                            for g in range(GC):
                                MM(PS[:, 2 + g, b * TS:(b + 1) * TS], STS[:, b, g, :], RF[:, g, b * TS:(b + 1) * TS], start=False, stop=False, skip_group_check=True)
                        pe.wait_ge(sem("state_rhs_out"), l + 1)
                        T1F = T1[:].rearrange("p h n -> p (h n)")
                        for g in range(GC):
                            end = turn(PS[:, 0, g * P:(g + 1) * P], T1F[:, g * P:(g + 1) * P])
                        end.then_inc(sem("rhs_in"), 1)
                        pe.wait_ge(sem("rhs_ready"), l * (PT * NCH + 1) + PT * NCH + 1)
                        for h, g, e, hc, pr in heads():
                            end = MM(PS[:, 1, hc], XTR[:, h, :], RH[:, hc], start=True, stop=True)
                        end.then_inc(sem("u_in"), 1)
                        pe.wait_ge(sem("u_done"), l * (PT * NCH + 1) + PT * NCH + 1)
                        for h, g, e, hc, pr in heads():
                            end = MM(PS[pr, 2 + g, 0:P], NU[:, hc], LTG[:, h, 1, :], start=False, stop=True, skip_group_check=True)
                        end.then_inc(sem("yr_in"), 1)
                        for h, g, e, hc, pr in heads():
                            gc = slice(g * P, (g + 1) * P)
                            pe.wait_ge(sem("spread_u"), l * NH + h + 1)
                            MM(PS[:, 4 + h, :], TOK[:, 0, gc], NM[:, 0].rearrange("p b n -> p (b n)"), start=True, stop=False)
                            MM(PS[:, 4 + h, :], TOK[:, 1, gc], NM[:, 1].rearrange("p b n -> p (b n)"), start=False, stop=True).then_inc(sem("sample_delta"), 1)
                        pe.wait_ge(sem("sample_states"), l + 1)
                        pe.wait_ge(sem("yr_out"), q + 1)
                        for b in range(NSTR):
                            for g in range(GC):
                                at = (b * GC + g) * P
                                end = turn(PSF[:, at:at + P], STS[:, b, g, :])
                        end.then_inc(sem("sample_state_in"), 1)
                pe.wait_ge(sem("sample_state_out"), l + 1)
                head_sums(CSP, 0).then_inc(sem("mean_in"), 1)
                pe.wait_ge(sem("centred"), l + 1)
                head_sums(SCR, 2).then_inc(sem("var_in"), 1)

                with pe.Fori(0, DC // 2) as i:
                    for m in (0, 1):
                        p = l * 3 + 1
                        pe.wait_ge(sem("mixed"), l + 1)
                        pe.wait_ge(sem("y_copied"), 1 + p * DC + i * 2 + m)
                        from_h(m, m, base(l, m, 1) + ((NW + 1) // 2, NW // 2)[m] + i, p, False)
                postnorm(l * 3 + 1)
                prenorm(l * 3 + 2)
                ffn(l, 1)
            pe.wait_ge(sem("x_ready"), (DEPTH * 3 + 1) * DC)
            for i in range(TT):
                if i >= 2:
                    pe.wait_ge(sem("out_rows"), i - 1)
                for c in range(DC):
                    at = (i % 2) * 1024 + c * P
                    end = turn(PSF[:, at:at + P], XT[:, c, i * P:(i + 1) * P])
                end.then_inc(sem("rows_in"), 1)


_INS = ["x_prompt", "x_sample", "cache_sb_k", "cache_sb_v", "state_wkv", "state_shift", "state_conv", "state_pool",
        "norm_g", "ffn_w_gate", "ffn_w_up", "ffn_w_down", "w_in", "w_out", "pool_w", "pool_scale", "rwkv_mu",
        "rwkv_w0", "rwkv_w2", "rwkv_a0", "rwkv_a2", "rwkv_g2", "rwkv_k_k", "rwkv_k_a", "rwkv_r_k", "rwkv_ln_w",
        "rwkv_ln_b", "conv_w"]
_OUTS = [("y_prompt", (1, TP, D)), ("y_sample", (NSTR, TS, D)),
         ("p_sb_k", (DEPTH, 1, TP, NH, HD)), ("p_sb_v", (DEPTH, 1, TP, NH, HD)),
         ("p_wkv", (DEPTH, 1, NH, HD, HD)), ("p_shift", (DEPTH, 1, RWKV_IN)),
         ("p_conv", (DEPTH, 1, CONV_W - 1, G)), ("p_pool", (DEPTH, 1, POOL_ST, G)),
         ("s_sb_k", (DEPTH, NSTR, TS, NH, HD)), ("s_sb_v", (DEPTH, NSTR, TS, NH, HD)),
         ("s_wkv", (DEPTH, NSTR, NH, HD, HD)), ("s_shift", (DEPTH, NSTR, RWKV_IN)),
         ("s_conv", (DEPTH, NSTR, CONV_W - 1, G)), ("s_pool", (DEPTH, NSTR, POOL_ST, G))]


def kernel(**inputs):
    import concourse.bacc as _bacc
    import numpy as _np
    from concourse.bass_utils import run_bass_kernel_spmd as _run

    nc = _bacc.Bacc("TRN2", target_bir_lowering=False, num_devices=1)
    arrays, io = {}, {}
    for name in _INS:
        a = _np.ascontiguousarray(inputs[name])
        arrays[f"in_{name}"] = a
        io[name] = nc.dram_tensor(f"in_{name}", a.shape, mybir.dt.from_np(a.dtype), kind="ExternalInput").ap()
    arrays["in_consts"] = constants(_np)
    io["consts"] = nc.dram_tensor("in_consts", (P, NCON), F32, kind="ExternalInput").ap()
    for name, shape in _OUTS:
        io[name] = nc.dram_tensor(f"out_{name}", shape, F32, kind="ExternalOutput").ap()
    build(nc, io)
    r = _run(nc, [arrays], core_ids=[0])
    return tuple(r.results[0][f"out_{name}"] for name, _ in _OUTS)
```

```python
import math
from contextlib import ExitStack

import concourse.bass as bass
from concourse import mybir
from concourse.alu_op_type import AluOpType as ALU

F32 = mybir.dt.float32
F32R = mybir.dt.float32r
ACT = mybir.ActivationFunctionType

P = 128
DEPTH, D, TP, NSTR, TS, PAST = 2, 1024, 512, 8, 16, 128
T = TP + NSTR * TS
TT = T // P
PT = TP // P
HALF = T // 2
DC = D // P
G = D // 4
GC = G // P
NH, HD = 4, 64
FF = 2816
FT = FF // P
RANKS = (32, 32, 64)
RWKV_IN = 3 * G + sum(RANKS)
RC = RWKV_IN // P
POOL_ST, CONV_W = 15, 3
SLOTS = 8
CH = 64
NCH = P // CH
DECAY = math.exp(-0.5)
EPS, GN_EPS = 1e-6, 64e-5

W_RWKV = [8, 4, 5, 2, 3, 6, 7]
W_SB = [15, 16, 17, 18, 19, 20]
W_CONV = [9, 10, 11, 12, 13, 14]
W_POOL = [0, 1]
W_TILES = W_RWKV + W_CONV + W_POOL + W_SB
NW = len(W_TILES)
STATES_AT, DECAY_AT, A_AT, GATE_AT, KK_AT, BONUS_AT, TAILS_AT = 1, 3, 5, 7, 9, 11, 17

DOWN_CUTS = [(0, 8), (8, 15), (15, 22)]
FFN_BLOCKS = FT + len(DOWN_CUTS) * DC // 2
MIX_BLOCKS = [(NW + 1) // 2 + DC // 2, NW // 2 + DC // 2]
LAYER_BLOCKS = [2 * FFN_BLOCKS + m for m in MIX_BLOCKS]

VEC = {}
for _n, _c in (("norm_g", 6 * DC), ("pool_scale", GC), ("mu", RC), ("w0", GC), ("a0", GC), ("k_k", GC),
               ("k_a", GC), ("r_k", GC), ("ln_w", GC), ("ln_b", GC), ("conv_w", CONV_W * GC)):
    VEC[_n] = (sum(c for _, c in VEC.values()), _c)
NV = sum(c for _, c in VEC.values())

CON = {}
for _n, _c in (("ident", P), ("ones", P), ("headones", P), ("see_prompt", P), ("see_sample", P),
               ("reset", T), ("icnt", GC * 16), ("iw", GC),
               ("tri_prompt", 2 * P), ("tri_sample", 2 * P), ("level1", P), ("levels", 6 * P),
               ("rowmask", NSTR)):
    CON[_n] = (sum(c for _, c in CON.values()), _c)
NCON = sum(c for _, c in CON.values())
KEPT = CON["reset"][0]


def constants(np):
    t = np.zeros((P, NCON), np.float32)

    def put(name, a):
        at, n = CON[name]
        t[:, at:at + n] = a.reshape(P, n)

    i, j = np.arange(P)[:, None], np.arange(P)[None, :]
    put("ident", (i == j) * 1.0)
    put("ones", np.ones((P, P)))
    put("headones", (i // HD == j // HD) * 1.0)
    put("see_prompt", np.where(j < i, 0.0, -1e30))
    put("see_sample", np.where((j < i) & (i // TS == j // TS), 0.0, -1e30))
    tok = np.arange(T)
    put("reset", np.tile(np.where(tok < TP, tok % CH != 0, (tok - TP) % TS != 0) * 1.0, (P, 1)))
    win = np.array([[2, 8], [4, 16]])[np.arange(P) // 64]
    put("iw", 1.0 / win)
    put("icnt", 1.0 / np.minimum(win[:, :, None], np.arange(16)[None, None, :] + 1))
    for name, b in (("tri_prompt", CH), ("tri_sample", TS)):
        same = i // b == j // b
        put(name, np.stack([(i < j) & same, (i <= j) & same], 1) * 1.0)
    put("level1", ((i // 2 == j // 2) & (i > j)) * 1.0)
    put("levels", np.stack([(i // (2 * b) == j // (2 * b)) & (i // b < j // b) for b in (1, 2, 4, 8, 16, 32)], 1) * 1.0)
    put("rowmask", (i // TS == np.arange(NSTR)[None, :]) * 1.0)
    return t


SAMPLE_LEVELS, PROMPT_LEVELS = 3, 5
UNITS = (PT + 1) * NH


def levels_before(l, tt):
    return l * (PT * PROMPT_LEVELS + SAMPLE_LEVELS) + tt * PROMPT_LEVELS


def inner_levels_before(l, tt):
    return l * (PT * (PROMPT_LEVELS - 1) + SAMPLE_LEVELS - 1) + tt * (PROMPT_LEVELS - 1)



def build(nc, io):
    es = ExitStack()
    with es:
        sems = {}

        def sem(name):
            if name not in sems:
                sems[name] = es.enter_context(nc.semaphore(name))
            return sems[name]

        def sb(name, shape, dt=F32, stack=es):
            return stack.enter_context(nc.sbuf_tensor(name, shape, dt))

        XT = sb("xT", [P, DC, T])
        RAW = [sb(f"w_raw{s}", [P, SLOTS, P]) for s in (0, 1)]
        WSP = [sb(f"w_split{s}", [P, 2, SLOTS, P], F32R) for s in (0, 1)]
        SCR = sb("scratch", [P, 2, T])
        ACC = sb("square_sums", [P, T])
        CONS = sb("consts", [P, KEPT])
        VROW = sb("vec_rows", [NV, P])
        LV = sb("layer_vecs", [P, NV])
        KA1 = sb("one_minus_k_a", [P, GC])
        COLS = sb("token_cols", [P, TT])
        EPSC = sb("eps_cols", [P, 3])
        HCOLS = sb("token_head_cols", [P, TT * NH])
        SMALLW = sb("rank_weights", [P, G])
        scope = ExitStack()
        H = sb("h_split", [P, DC, 2, T], F32R, scope)
        scope.close()
        scope = ExitStack()
        Y = sb("y", [P, DC, T], stack=scope)
        scope.close()
        sb("h_region", [P, 2 * DC * T])
        scope = ExitStack()
        HID = sb("hidden_split", [P, FT, 2, T], F32R, scope)
        scope.close()
        scope = ExitStack()
        IO = sb("token_rows", [P, TT, D], stack=scope)
        scope.close()
        scope = ExitStack()
        YM = sb("y_mixer", [P, DC, T], stack=scope)
        scope.close()
        mix = ExitStack()
        XS = sb("xs", [P, RC, T], stack=mix)
        SBQ = sb("sb_qkv", [P, 6, T], stack=mix)
        CS = sb("decay_sum", [P, GC, T], stack=mix)
        CSP = sb("decay_sum_before", [P, GC, T], stack=mix)
        BA = sb("kk_a", [P, GC, T], stack=mix)
        KK = sb("kk", [P, GC, T], stack=mix)
        GA = sb("gate", [P, GC, T], stack=mix)
        BV = sb("bonus_v", [P, GC, T], stack=mix)
        scope = ExitStack()
        RWP = sb("rw_prompt", [P, RC, 1 + TP], stack=scope)
        RWS = sb("rw_sample", [P, RC, NSTR, 1 + TS], stack=scope)
        PBP = sb("pool_prompt", [P, GC, POOL_ST + TP], stack=scope)
        PBS = sb("pool_sample", [P, GC, NSTR, POOL_ST + TS], stack=scope)
        CV = sb("conv_in", [P, 6, T], stack=scope)
        ZP = sb("z_prompt", [P, GC, 2 + TP], stack=scope)
        ZS = sb("z_sample", [P, GC, NSTR, 2 + TS], stack=scope)
        RESET = sb("reset", [P, T], stack=scope)
        ICNT = sb("inv_counts", [P, GC, 16], stack=scope)
        IW = sb("inv_windows", [P, GC], stack=scope)
        scope.close()
        scope = ExitStack()
        VT = sb("v_rows", [P, TT, G], stack=scope)
        VC = sb("v_cache", [P, NSTR, G], stack=scope)
        KC = sb("k_cache", [P, NSTR, G], stack=scope)
        KCT = sb("k_cacheT", [P, GC, NSTR, PAST], stack=scope)
        QM = sb("q_masked", [P, GC, NSTR * (P + TS)], stack=scope)
        KE = sb("keep", [P, 2, TP + 8], stack=scope)
        AT = sb("attnT", [P, 2, 4, P], stack=scope)
        scope.close()
        scope = ExitStack()
        LTG = sb("beta_scores", [P, NH, 2, P], stack=scope)
        KTG = sb("kappa_scores", [P, NH, 2, P], stack=scope)
        X = sb("inv", [P, NH, P], stack=scope)
        XTR = sb("invT", [P, NH, P], stack=scope)
        NT = sb("level_blocks", [P, 2, NH, P], stack=scope)
        T1 = sb("level_product", [P, NH, P], stack=scope)
        AR = sb("alpha_rho_by_head", [P, 2, GC, 2, P], stack=scope)
        AFS = sb("alpha", [P, 2, GC, P], stack=scope)
        RFS = sb("rho", [P, 2, GC, P], stack=scope)
        PCS = sb("chunk_decay", [P, 2, GC, NSTR], stack=scope)
        BK = sb("beta_kappa", [P, 2, GC, P], stack=scope)
        TOK = sb("beta_kappa_v_rows", [P, 3, G], stack=scope)
        MVS = sb("mv", [P, G], stack=scope)
        RH = sb("rhs", [P, G], stack=scope)
        NU = sb("minus_u", [P, G], stack=scope)
        ST = sb("state_prompt", [P, GC, P], stack=scope)
        STS = sb("state_sample", [P, NSTR, GC, P], stack=scope)
        TRI = sb("triangles", [P, 2, P], stack=scope)
        LEV1 = sb("level1_mask", [P, P], stack=scope)
        LEV = sb("level_masks", [P, 6, P], stack=scope)
        ROWM = sb("row_masks", [P, NSTR], stack=scope)
        scope.close()
        mix.close()

        IDENT = CONS[:, CON["ident"][0]:CON["ident"][0] + P]
        ONES = CONS[:, CON["ones"][0]:CON["ones"][0] + P]
        HEADS = CONS[:, CON["headones"][0]:CON["headones"][0] + P]
        SEE = [CONS[:, CON[n][0]:CON[n][0] + P] for n in ("see_prompt", "see_sample")]
        PS = es.enter_context(nc.psum_tensor("ps", [P, 8, 512], F32))
        PSF = PS[:].rearrange("p b n -> p (b n)")

        def pset(q):
            return PS[:, 2 * q:2 * q + 2, 0:HALF]

        def halves(ap):
            return ap.rearrange("p (a n) -> p a n", a=2)

        def vec(name, c):
            return LV[:, VEC[name][0] + c:VEC[name][0] + c + 1]

        SGB, HB = SCR[:, 0, :], SCR[:, 1, :]
        SQR = [SCR[:, 0, :], SBQ[:, 1, :]]
        STIN = BV[:].rearrange("p g t -> p (g t)")[:, 0:RWKV_IN]
        STIN2 = KK[:].rearrange("p g t -> p (g t)")
        PW = ACC[:, 0:2 * P].rearrange("p (g n) -> p g n", g=2)
        CVF = CV[:].rearrange("p s t -> p (s t)")
        TAIL = SCR[:].rearrange("p s t -> p (s t)")
        OUTS = RWP[:].rearrange("p c t -> p (c t)")
        KT = SCR[:].rearrange("p s t -> p (s t)").rearrange("p (i n) -> p i n", i=TT)
        KCF = KC[:].rearrange("p b n -> p (b n)")
        SIG = KCF[:, 0:2 * TP].rearrange("p (s n) -> p s n", s=2)
        AW = KCF[:, 2 * TP:4 * TP].rearrange("p (s n) -> p s n", s=2)
        EXPS = SCR[:].rearrange("p s t -> p (s t)")[:, 0:3 * G].rearrange("p (k g n) -> p k g n", k=3, g=GC)
        BP = SCR[:].rearrange("p s t -> p (s t)")[:, 3 * G:5 * G].rearrange("p (k g n) -> p k g n", k=2, g=GC)
        SBF = SBQ[:].rearrange("p s t -> p (s t)")
        SN = SBF[:, 0:NSTR * G].rearrange("p (b g n) -> p b g n", b=NSTR, g=GC)
        at = NSTR * G
        NMU = [SBF[:, at + k * NSTR * HD:at + (k + 1) * NSTR * HD] for k in (0, 1)]
        NMK = [SBF[:, at + 2 * NSTR * HD:at + 3 * NSTR * HD], ACC[:, 0:NSTR * HD]]

        def by_stream(ap):
            return ap.rearrange("p (b n) -> p b n", b=NSTR)

        block = es.enter_context(nc.Block())

        def base(l, s, seg):
            return l * LAYER_BLOCKS[s] + (0, FFN_BLOCKS, FFN_BLOCKS + MIX_BLOCKS[s])[seg]

        w_in_v = io["w_in"].rearrange("l (c p) n -> l p c n", p=P)
        w_out_v = io["w_out"].rearrange("l (c p) n -> l p c n", p=P)
        w_gu_v = [io[n].rearrange("l f (c p) n -> l f p c n", p=P) for n in ("ffn_w_gate", "ffn_w_up")]
        w_dn_v = io["ffn_w_down"].rearrange("l f (c p) n -> l f p c n", p=P)

        @block.sync
        def _(sp):
            def load_block(s, k, src, n=SLOTS):
                sp.wait_ge(sem(f"hi_ready{s}"), k + 1)
                sp.wait_ge(sem(f"lo_ready{s}"), k + 1)
                sp.sem_inc(sem("slot_seen"), 1)
                sp.dma_start(RAW[s][:, 0:n, :], src).then_inc(sem(f"raw_loaded{s}"), 16)

            def load_ffn(l, f):
                k0, k1 = base(l, 0, 2 * f), base(l, 1, 2 * f)
                with sp.Fori(0, FT) as j:
                    load_block(0, k0 + j, w_gu_v[0][l, f, :, :, bass.ds(j * P, P)])
                    load_block(1, k1 + j, w_gu_v[1][l, f, :, :, bass.ds(j * P, P)])
                with sp.Fori(0, DC // 2) as i:
                    for m in (0, 1):
                        for b, (r0, r1) in enumerate(DOWN_CUTS):
                            q = m * 3 + b
                            load_block(q % 2, base(l, q % 2, 2 * f) + FT + i * 3 + q // 2,
                                       w_dn_v[l, f, :, r0:r1, bass.ds((i * 2 + m) * P, P)], r1 - r0)

            sp.dma_start(CONS[:], io["consts"][:, 0:KEPT]).then_inc(sem("consts_loaded"), 16)
            for i in range(TT):
                src = io["x_prompt"][0, i * P:(i + 1) * P, :] if i < PT else io["x_sample"].rearrange("b t n -> (b t) n")
                sp.dma_start(IO[:, i, :], src).then_inc(sem(f"x_loaded{i}"), 16)

            with sp.Fori(0, DEPTH) as l:
                sp.wait_ge(sem("vec_ready"), l + 1)
                for name, (r, n) in VEC.items():
                    src = io["norm_g" if name == "norm_g" else ("rwkv_" + name if name not in ("pool_scale", "conv_w") else name)][l]
                    if name in ("norm_g", "conv_w"):
                        src = src.rearrange("s (c p) -> s c p", p=P).rearrange("s c p -> (s c) p")
                    elif name == "r_k":
                        src = src.rearrange("h n -> (h n)").rearrange("(c p) -> c p", p=P)
                    else:
                        src = src.rearrange("(c p) -> c p", p=P)
                    sp.dma_start(VROW[r:r + n, :], src).then_inc(sem("vec_loaded"), 16)
                r = 0
                for name, n in zip(("rwkv_w2", "rwkv_a2", "rwkv_g2"), RANKS):
                    sp.dma_start(SMALLW[r:r + n, :], io[name][l]).then_inc(sem("rank_loaded"), 16)
                    r += n
                load_ffn(l, 0)
                k0, k1 = base(l, 0, 1), base(l, 1, 1)
                for t, w in enumerate(W_TILES):
                    load_block(t % 2, (k0, k1)[t % 2] + t // 2, w_in_v[l, :, :, w * P:(w + 1) * P])
                    if t == 1:
                        sp.wait_ge(sem("y_added"), 1 + (l * 3 + 1) * DC)
                        sp.dma_start(STIN[0:NSTR, :], io["state_shift"][l]).then_inc(sem("state_loaded"), 16)
                        sp.dma_start(STIN2[0:2 * NSTR, 0:G], io["state_conv"][l].rearrange("b t n -> (b t) n")).then_inc(sem("state_loaded"), 16)
                        sp.dma_start(STIN2[0:POOL_ST * NSTR, G:2 * G], io["state_pool"][l].rearrange("b t n -> (b t) n")).then_inc(sem("state_loaded"), 16)
                        for dst, name in ((RESET[:], "reset"), (ICNT[:].rearrange("p g n -> p (g n)"), "icnt"), (IW[:], "iw")):
                            at, n = CON[name]
                            sp.dma_start(dst, io["consts"][:, at:at + n]).then_inc(sem("tables_loaded"), 16)
                    if t == 5:
                        sp.wait_ge(sem("poolw_zeroed"), l + 1)
                        for g in range(2):
                            for e in range(2):
                                sp.dma_start(PW[64 * e:64 * e + 64, g, 64 * e:64 * e + 64], io["pool_w"][l, 2 * g + e]).then_inc(sem("poolw_loaded"), 16)
                kb = ((NW + 1) // 2, NW // 2)
                for m in (0, 1):
                    load_block(m, (k0, k1)[m] + kb[m], w_out_v[l, :, :, m * P:(m + 1) * P])
                sp.wait_ge(sem("tails_out"), l + 1)
                sp.dma_start(io["p_shift"][l], OUTS[0:1, 0:RWKV_IN]).then_inc(sem("tails_stored"), 16)
                sp.dma_start(io["s_shift"][l], OUTS[1:1 + NSTR, 0:RWKV_IN]).then_inc(sem("tails_stored"), 16)
                sp.dma_start(io["p_conv"][l, 0], OUTS[0:2, 896:896 + G]).then_inc(sem("tails_stored"), 16)
                sp.dma_start(io["s_conv"][l].rearrange("b t n -> (b t) n"), OUTS[2:2 + 2 * NSTR, 896:896 + G]).then_inc(sem("tails_stored"), 16)
                sp.dma_start(io["s_pool"][l].rearrange("b t n -> (b t) n"), OUTS[0:NSTR * POOL_ST, 1152:1152 + G]).then_inc(sem("tails_stored"), 16)
                sp.dma_start(io["p_pool"][l, 0], OUTS[0:POOL_ST, 1408:1408 + G]).then_inc(sem("tails_stored"), 16)
                sp.wait_ge(sem("attn_region"), l + 1)
                sp.dma_start(KC[:], io["cache_sb_k"][l].rearrange("b s h n -> s b (h n)")).then_inc(sem("kc_loaded"), 16)
                sp.dma_start(VC[:], io["cache_sb_v"][l].rearrange("b s h n -> s b (h n)")).then_inc(sem("vc_loaded"), 16)
                sp.wait_ge(sem("kv_out"), (l + 1) * TT)
                for src, a, b in ((KT, "p_sb_k", "s_sb_k"), (VT, "p_sb_v", "s_sb_v")):
                    sp.dma_start(io[a][l, 0].rearrange("(i p) h n -> p i (h n)", p=P), src[:, 0:PT, :]).then_inc(sem("kv_stored"), 16)
                    sp.dma_start(io[b][l].rearrange("b t h n -> (b t) (h n)"), src[:, PT, :]).then_inc(sem("kv_stored"), 16)
                sp.wait_ge(sem("attn_over"), l + 1)
                for dst, name in ((TRI[:].rearrange("p a n -> p (a n)"), "tri_prompt"), (LEV1[:], "level1"),
                                  (LEV[:].rearrange("p a n -> p (a n)"), "levels"), (ROWM[:], "rowmask")):
                    at, n = CON[name]
                    sp.dma_start(dst, io["consts"][:, at:at + n]).then_inc(sem("masks_loaded"), 16)
                sp.wait_ge(sem("states_zeroed"), l + 1)
                wkv_in = io["state_wkv"][l].rearrange("b (g e) v k -> e v b g k", e=2)
                for g in range(2):
                    for e in range(2):
                        sp.dma_start(SN[64 * e:64 * e + 64, :, g, 64 * e:64 * e + 64], wkv_in[e, :, :, g, :]).then_inc(sem("wkv_loaded"), 16)
                sp.wait_ge(sem("scores_masked"), l * TT + PT)
                at, n = CON["tri_sample"]
                sp.dma_start(TRI[:].rearrange("p a n -> p (a n)"), io["consts"][:, at:at + n]).then_inc(sem("sample_tri_loaded"), 16)
                sp.wait_ge(sem("prompt_state_out"), l + 1)
                for g in range(2):
                    for e in range(2):
                        sp.dma_start(io["p_wkv"][l, 0, 2 * g + e], ST[64 * e:64 * e + 64, g, 64 * e:64 * e + 64]).then_inc(sem("wkv_stored"), 16)
                sp.wait_ge(sem("sample_state_out"), l + 1)
                wkv_out = io["s_wkv"][l].rearrange("b (g e) v k -> e v b g k", e=2)
                for g in range(2):
                    for e in range(2):
                        sp.dma_start(wkv_out[e, :, :, g, :], SN[64 * e:64 * e + 64, :, g, 64 * e:64 * e + 64]).then_inc(sem("wkv_stored"), 16)
                for m in range(2, DC):
                    load_block(m % 2, (k0, k1)[m % 2] + kb[m % 2] + m // 2, w_out_v[l, :, :, m * P:(m + 1) * P])
                load_ffn(l, 1)
            for s in (0, 1):
                load_block(s, DEPTH * LAYER_BLOCKS[s], w_gu_v[0][0, 0, :, :, 0:P])
            for i in range(TT):
                sp.wait_ge(sem("out_rows"), i + 1)
                dst = io["y_prompt"][0, i * P:(i + 1) * P, :] if i < PT else io["y_sample"].rearrange("b t n -> (b t) n")
                sp.dma_start(dst, IO[:, i, :]).then_inc(sem("y_stored"), 16)
            sp.wait_ge(sem("tails_stored"), DEPTH * 6 * 16)
            sp.wait_ge(sem("kv_stored"), DEPTH * 4 * 16)
            sp.wait_ge(sem("wkv_stored"), DEPTH * 8 * 16)
            sp.wait_ge(sem("y_stored"), TT * 16)
            for s in (0, 1):
                sp.wait_ge(sem(f"raw_loaded{s}"), 16 * (DEPTH * LAYER_BLOCKS[s] + 1))

        @block.gpsimd
        def _(pool):
            def low(s, k):
                pool.wait_ge(sem(f"hi_ready{s}"), k + 2)
                nc.gpsimd.tensor_tensor(WSP[s][:, 1], RAW[s][:], WSP[s][:, 0].bitcast(F32), ALU.subtract).then_inc(sem(f"lo_ready{s}"), 1)

            for s in (0, 1):
                pool.sem_inc(sem(f"lo_ready{s}"), 1)
            def sum_squares(p):
                for k in range(1, DC):
                    pool.wait_ge(sem("squares"), p * DC + k + 1)
                    nc.gpsimd.tensor_tensor(ACC[:], ACC[:], SQR[k % 2], ALU.add)
                    pool.drain().then_inc(sem("squares_summed"), 1)

            with pool.Fori(0, DEPTH) as l:
                for s in (0, 1):
                    low(s, base(l, s, 0))
                sum_squares(l * 3)
                with pool.Fori(1, FFN_BLOCKS) as b:
                    low(0, base(l, 0, 0) + b)
                    low(1, base(l, 1, 0) + b)
                for s in (0, 1):
                    low(s, base(l, s, 1))
                sum_squares(l * 3 + 1)
                with pool.Fori(1, NW // 2) as b:
                    low(0, base(l, 0, 1) + b)
                    low(1, base(l, 1, 1) + b)
                low(0, base(l, 0, 1) + NW // 2)
                low(1, base(l, 1, 1) + NW // 2)
                low(0, base(l, 0, 1) + (NW + 1) // 2)
                for tt in range(TT):
                    q = l * TT + tt
                    nlev = SAMPLE_LEVELS if tt == PT else PROMPT_LEVELS
                    lev0 = levels_before(l, tt)
                    pool.wait_ge(sem("lt_ready"), q + 1)
                    for v in range(1, nlev):
                        if v >= 2:
                            pool.wait_ge(sem("t1_in1"), lev0 + v - 1)
                        nc.gpsimd.tensor_tensor(NT[:, v % 2], LTG[:, :, 0, :], LEV[:, v + 1, :].unsqueeze(1).broadcast_to([P, NH, P]), ALU.mult).then_inc(sem("blocks_ready"), 1)
                pool.wait_ge(sem("rows_ready"), (l + 1) * TT)
                for h in range(NH):
                    if h >= 2:
                        pool.wait_ge(sem("sample_delta"), l * NH + h - 1)
                    nc.gpsimd.tensor_tensor(by_stream(NMK[h % 2]), TOK[:, 2, h * HD:(h + 1) * HD].unsqueeze(1).broadcast_to([P, NSTR, HD]),
                                            ROWM[:].unsqueeze(2).broadcast_to([P, NSTR, HD]), ALU.mult).then_inc(sem("kappa_spread"), 1)
                with pool.Fori(1, DC // 2) as b:
                    low(0, base(l, 0, 1) + (NW + 1) // 2 + b)
                    low(1, base(l, 1, 1) + NW // 2 + b)
                for s in (0, 1):
                    low(s, base(l, s, 2))
                sum_squares(l * 3 + 2)
                with pool.Fori(1, FFN_BLOCKS) as b:
                    low(0, base(l, 0, 2) + b)
                    low(1, base(l, 1, 2) + b)

        @block.scalar
        def _(act):
            A = nc.scalar.activation

            def round_weights(s, k):
                act.wait_ge(sem(f"raw_loaded{s}"), 16 * (k + 1))
                act.wait_ge(sem(f"block_used{s}"), k)
                A(WSP[s][:, 0], RAW[s][:], ACT.Copy).then_inc(sem(f"hi_ready{s}"), 1)

            def after_block(s, k):
                act.wait_ge(sem(f"block_used{s}"), k + 1)
                round_weights(s, k + 1)

            def x_high(c, gain):
                A(H[:, c, 0, :], XT[:, c, :], ACT.Copy, scale=vec("norm_g", gain + c)).then_inc(sem("h_hi"), 1)

            def x_squares(p, gain=None, late=None):
                for k in range(DC):
                    c = DC - 1 - k
                    act.wait_ge(sem("x_ready"), p * DC + k + 1)
                    if gain is not None and late is None:
                        x_high(c, gain)
                    if k >= 3:
                        act.wait_ge(sem("squares_summed"), p * (DC - 1) + k - 2)
                    A(SQR[k % 2] if k else ACC[:], XT[:, c, :], ACT.Square).then_inc(sem("squares"), 1)
                if late is not None:
                    act.wait_ge(sem("vec_ready"), late + 2)
                    for c in reversed(range(DC)):
                        x_high(c, gain)
                act.wait_ge(sem("pre_summed"), p + 1)
                A(COLS[:], PS[:, 7, 0:TT], ACT.Sqrt, bias=EPSC[:, 0:1], scale=1.0 / D).then_inc(sem("pre_root"), 1)

            def prenorm(l, p):
                x_squares(p)
                for c in range(DC):
                    act.wait_ge(sem("h_full"), l * DC + c + 1)
                    A(H[:, c, 0, :], SCR[:, c % 2, :], ACT.Copy).then_inc(sem("h_hi"), 1)

            def y_tiles(p, blocks, Y=Y):
                with act.Fori(0, DC // 2) as i:
                    for m in (0, 1):
                        blk = blocks(i, m)
                        for s, k in blk[:-1]:
                            after_block(s, k)
                        s, k = blk[-1]
                        after_block(s, k)
                        act.wait_ge(sem("y_copied"), 3 + p * DC + i * 2 + m)
                        act.wait_ge(sem("y_added"), 1 + p * DC + i * 2 + m)
                        A(SGB, Y[:, i * 2 + m, :], ACT.Square).then_inc(sem("y_squares"), 1)

            def postnorm(p, half):
                act.wait_ge(sem("post_summed"), p + 1)
                four = 4.0 if half else 1.0
                A(COLS[:], PS[:, 7, 0:TT], ACT.Sqrt, bias=EPSC[:, 1:2] if half else EPSC[:, 0:1], scale=four / D).then_inc(sem("post_root"), 1)

            def ffn(l, f):
                n = l * 2 + f
                with act.Fori(0, FT // 2) as i:
                    for jj in (0, 1):
                        j = i * 2 + jj
                        k0, k1 = base(l, 0, 2 * f) + j, base(l, 1, 2 * f) + j
                        after_block(0, k0)
                        act.wait_ge(sem("gate_scaled"), 3 + n * FT + j)
                        A(SGB, SGB, ACT.Silu).then_inc(sem("silu"), 1)
                        after_block(1, k1)
                        act.wait_ge(sem("hidden"), 1 + n * FT + j)
                        A(HID[:, j, 0, :], HB, ACT.Copy).then_inc(sem("hidden_hi"), 1)
                y_tiles(l * 3 + 2 * f, lambda i, m: [((m * 3 + b) % 2, base(l, (m * 3 + b) % 2, 2 * f) + FT + i * 3 + (m * 3 + b) // 2) for b in range(3)])
                postnorm(l * 3 + 2 * f, True)

            act.wait_ge(sem("zeroed"), 1)
            act.sem_inc(sem("u_out"), 2)
            for s in (0, 1):
                act.sem_inc(sem(f"hi_ready{s}"), 1)
            round_weights(0, 0)
            round_weights(1, 0)
            with act.Fori(0, DEPTH) as l:
                x_squares(l * 3, 0, late=l)
                ffn(l, 0)
                prenorm(l, l * 3 + 1)
                for t, w in enumerate(W_TILES):
                    k = base(l, t % 2, 1) + t // 2
                    act.wait_ge(sem(f"block_used{t % 2}"), k + 1)
                    src = pset(t % 2)
                    if w in W_RWKV or w in W_POOL:
                        c, pre = (w - GC, 1) if w in W_RWKV else (w, POOL_ST)
                        dp, ds = (RWP, RWS) if w in W_RWKV else (PBP, PBS)
                        A(dp[:, c, pre:pre + HALF], src[:, 0, :], ACT.Copy)
                        A(dp[:, c, pre + HALF:pre + TP], src[:, 1, 0:TP - HALF], ACT.Copy)
                        A(ds[:, c, :, pre:], src[:, 1, TP - HALF:HALF].rearrange("p (b t) -> p b t", b=NSTR), ACT.Copy).then_inc(sem("u_out"), 1)
                    else:
                        dst = SBQ[:, w - W_SB[0], :] if w in W_SB else CV[:, w - W_CONV[0], :]
                        A(halves(dst), src, ACT.Copy).then_inc(sem("u_out"), 1)
                    round_weights(t % 2, k + 1)
                    if t == DECAY_AT - 1:
                        act.wait_ge(sem("ranks_shifted"), l + 1)
                        A(XS[0:32, 6, :], XS[0:32, 6, :], ACT.Tanh)
                        A(XS[64:128, 6, :], XS[64:128, 6, :], ACT.Sigmoid)
                        act.drain().then_inc(sem("gates_ready"), 1)
                    if t == DECAY_AT:
                        act.wait_ge(sem("decay_in"), l + 1)
                        for o in range(GC):
                            A(halves(CS[:, o, :]), pset(2 + o), ACT.Sigmoid, bias=vec("w0", o))
                        act.drain().then_inc(sem("decay_ready"), 1)
                    if t == A_AT:
                        act.wait_ge(sem("a_in"), l + 1)
                        for o in range(GC):
                            A(halves(BA[:, o, :]), pset(2 + o), ACT.Sigmoid, bias=vec("a0", o))
                        act.drain().then_inc(sem("a_ready"), 1)
                    if t == GATE_AT:
                        act.wait_ge(sem("gate_in"), l + 1)
                        for o in range(GC):
                            A(halves(GA[:, o, :]), pset(2 + o), ACT.Copy)
                        act.drain().then_inc(sem("gate_ready"), 1)
                    if t == KK_AT:
                        act.wait_ge(sem("kk_summed"), l + 1)
                        A(SCR[:].rearrange("p g (a n) -> p (g a) n", a=2), PS[:, 4:8, 0:HALF], ACT.Sqrt).then_inc(sem("kk_root"), 1)
                act.wait_ge(sem("conv_ready"), l + 1)
                A(H[:, 4:6, 0, :], CV[:, 4:6, :], ACT.Copy).then_inc(sem("conv_hi"), 1)
                act.wait_ge(sem("pool_out"), l + 1)
                for g in range(GC):
                    A(halves(H[:, g, 0, :]), pset(2 + g), ACT.Copy, scale=vec("pool_scale", g))
                act.drain().then_inc(sem("pool_hi"), 1)

                act.wait_ge(sem("attn_region"), l + 1)
                for i in range(TT):
                    act.wait_ge(sem("kv_turned"), l * TT + i + 1)
                    A(KT[:, i, :], PS[:, i % 2, 0:G], ACT.Copy)
                    A(VT[:, i, :], PS[:, i % 2, G:2 * G], ACT.Copy)
                    act.drain().then_inc(sem("kv_out"), 1)
                act.wait_ge(sem("kc_turned"), l + 1)
                A(KCT[:].rearrange("p g b n -> p (g b n)"), PSF[:, 1024:3072], ACT.Copy).then_inc(sem("kcT_out"), 1)

                def attnT_out(u):
                    act.wait_ge(sem("attn_turned"), l * UNITS + u + 1)
                    if u >= 2:
                        act.wait_ge(sem("attn_done"), l * UNITS + u - 1)
                    nb = (u // NH + 1) if u < PT * NH else 2
                    A(AT[:, u % 2, 0:nb, :], PS[:, 2 + u % 2, 0:nb * P].rearrange("p (b n) -> p b n", b=nb), ACT.Copy).then_inc(sem("attnT_out"), 1)

                for u in range(UNITS + 1):
                    if u < UNITS:
                        n = P * (u // NH + 1) if u < PT * NH else 2 * P
                        act.wait_ge(sem("z_ready"), l * UNITS + u + 1)
                        if u >= 2:
                            act.wait_ge(sem("attn_ready"), l * UNITS + u - 1)
                        A(KE[:, u % 2, 0:n], PS[:, u % 2, 0:n], ACT.Sigmoid, scale=-HD ** -0.5)
                        A(SIG[:, u % 2, 0:n], PS[:, u % 2, 0:n], ACT.Sigmoid, scale=HD ** -0.5)
                        act.drain().then_inc(sem("sig_ready"), 1)
                    if u >= 1:
                        attnT_out(u - 1)
                act.wait_ge(sem("kv_stored"), (l + 1) * 4 * 16)

                def exps(tt):
                    ts = slice(tt * P, (tt + 1) * P)
                    A(EXPS[:, 0], CS[:, :, ts], ACT.Exp, scale=-DECAY)
                    A(EXPS[:, 1], CS[:, :, ts], ACT.Exp, scale=DECAY)
                    A(EXPS[:, 2], CSP[:, :, ts], ACT.Exp, scale=-DECAY)
                    act.drain().then_inc(sem("exps_ready"), 1)

                exps(0)
                act.wait_ge(sem("attn_done"), (l + 1) * UNITS)
                A(H[:, 6:8, 0, 0:TP], PS[:, 4:6, :], ACT.Copy)
                A(H[:, 6:8, 0, TP:T], PS[:, 6:8, 0:P], ACT.Copy)
                act.drain().then_inc(sem("attn_hi"), 1)

                for tt in range(TT):
                    q = l * TT + tt
                    sample = tt == PT
                    ts = slice(tt * P, (tt + 1) * P)
                    act.wait_ge(sem("scores_in"), q + 1)
                    A(TOK[:, 0:2, :], PS[:, 5, :].rearrange("p (k n) -> p k n", k=2), ACT.Copy)
                    A(TOK[:, 2, :], PS[:, 6, 0:G], ACT.Copy)
                    act.drain().then_inc(sem("rows_ready"), 1)
                    if not sample:
                        exps(tt + 1)
                    for v in range(SAMPLE_LEVELS if sample else PROMPT_LEVELS):
                        for a in (0, 1):
                            act.wait_ge(sem(f"t1_in{a}"), levels_before(l, tt) + v + 1)
                            A(T1[:, 2 * a:2 * a + 2, :], PS[:, 4 + 2 * a, 0:256].rearrange("p (h n) -> p h n", h=2), ACT.Copy).then_inc(sem(f"t1_out{a}"), 1)
                    if not sample:
                        for c in range(NCH):
                            act.wait_ge(sem("u_in"), l * (PT * NCH + 1) + tt * NCH + c + 1)
                            A(NU[64 * c:64 * c + 64, :], PS[64 * c:64 * c + 64, 1, 0:G], ACT.Copy, scale=-1.0).then_inc(sem("u_done"), 1)
                    else:
                        act.wait_ge(sem("stateT_in"), l + 1)
                        A(STS[:].rearrange("p b g n -> p (b g n)"), PSF[:, 0:2048], ACT.Copy).then_inc(sem("stateT_out"), 1)
                        act.wait_ge(sem("state_rhs_in"), l + 1)
                        A(T1[:].rearrange("p h n -> p (h n)")[:, 0:G], PS[:, 4, 0:G], ACT.Copy).then_inc(sem("state_rhs_out"), 1)
                        act.wait_ge(sem("u_in"), l * (PT * NCH + 1) + PT * NCH + 1)
                        A(NU[:, :], PS[:, 1, 0:G], ACT.Copy, scale=-1.0).then_inc(sem("u_done"), 1)
                    act.wait_ge(sem("yr_in"), q + 1)
                    A(CSP[:, :, ts], PS[:, 2:4, 0:P], ACT.Copy).then_inc(sem("yr_out"), 1)
                    if tt == PT - 1:
                        act.wait_ge(sem("prompt_state_in"), l + 1)
                        A(ST[:], PS[:, 4, 0:G].rearrange("p (g n) -> p g n", g=2), ACT.Copy).then_inc(sem("prompt_state_out"), 1)
                    if sample:
                        act.wait_ge(sem("sample_state_in"), l + 1)
                        A(SBF[:, 0:2048], PSF[:, 0:2048], ACT.Copy).then_inc(sem("sample_state_out"), 1)
                act.wait_ge(sem("var_in"), l + 1)
                A(HCOLS[:], PS[:, 4, 0:TT * NH], ACT.Sqrt, bias=EPSC[:, 2:3], scale=1.0 / HD).then_inc(sem("var_root"), 1)
                act.wait_ge(sem("yr_ready"), l + 1)
                A(H[:, 2:4, 0, :], SCR[:], ACT.Copy).then_inc(sem("yr_hi"), 1)

                y_tiles(l * 3 + 1, lambda i, m: [(m, base(l, m, 1) + ((NW + 1) // 2, NW // 2)[m] + i)], YM)
                postnorm(l * 3 + 1, False)
                x_squares(l * 3 + 2, 4 * DC)
                ffn(l, 1)
            for i in range(TT):
                act.wait_ge(sem("rows_in"), i + 1)
                A(IO[:, i, :], PSF[:, (i % 2) * 1024:(i % 2) * 1024 + 1024], ACT.Copy).then_inc(sem("out_rows"), 1)

        @block.vector
        def _(dve):
            V = nc.vector
            fence = dve.drain

            def prenorm(p):
                dve.wait_ge(sem("pre_root"), p + 1)
                rstd_rows()
                dve.wait_ge(sem("pre_spread"), p + 1)

                def full(c):
                    V.scalar_tensor_tensor(out=SCR[:, c % 2, :], in0=XT[:, c, :], scalar=vec("norm_g", norm_index + c),
                                           in1=PSF[:, 2048:2048 + T], op0=ALU.mult, op1=ALU.mult).then_inc(sem("h_full"), 1)

                full(0)
                for c in range(DC):
                    if c + 1 < DC:
                        full(c + 1)
                    fence()
                    dve.wait_ge(sem("h_hi"), p * DC + c + 1)
                    V.tensor_tensor(H[:, c, 1, :], SCR[:, c % 2, :], H[:, c, 0, :].bitcast(F32), ALU.subtract)
                    fence().then_inc(sem("h_ready"), 1)

            def rstd_rows():
                V.reciprocal(COLS[:], COLS[:])
                fence()
                V.tensor_tensor(ACC[:].rearrange("p (i n) -> p i n", i=TT), IDENT.unsqueeze(1).broadcast_to([P, TT, P]),
                                COLS[:].unsqueeze(2).broadcast_to([P, TT, P]), ALU.mult).then_inc(sem("diagonals"), 1)

            def y_tiles(p, blocks, Y=Y):
                V.memset(ACC[:], 0.0)
                fence()
                with dve.Fori(0, DC // 2) as i:
                    for m in (0, 1):
                        s, k = blocks(i, m)[-1]
                        dve.wait_ge(sem(f"block_used{s}"), k + 1)
                        V.tensor_copy(halves(Y[:, i * 2 + m, :]), pset(m)).then_inc(sem("y_copied"), 1)
                        dve.wait_ge(sem("y_squares"), 1 + p * DC + i * 2 + m)
                        V.tensor_tensor(ACC[:], ACC[:], SGB, ALU.add)
                        fence().then_inc(sem("y_added"), 1)

            def h_low(p, k, gain):
                c = DC - 1 - k
                dve.wait_ge(sem("h_hi"), p * DC + k + 1)
                V.scalar_tensor_tensor(out=H[:, c, 1, :], in0=XT[:, c, :], scalar=vec("norm_g", gain + c), in1=H[:, c, 0, :].bitcast(F32),
                                       op0=ALU.mult, op1=ALU.subtract).then_inc(sem("h_ready"), 1)

            def postnorm(p, Y=Y, gain=None):
                dve.wait_ge(sem("post_root"), p + 1)
                rstd_rows()
                dve.wait_ge(sem("post_spread"), p + 1)
                for k in range(DC):
                    c = DC - 1 - k
                    V.tensor_tensor(HB, Y[:, c, :], PSF[:, 2048:2048 + T], ALU.mult)
                    fence()
                    V.scalar_tensor_tensor(out=XT[:, c, :], in0=HB, scalar=vec("norm_g", norm_index + c), in1=XT[:, c, :],
                                           op0=ALU.mult, op1=ALU.add)
                    fence().then_inc(sem("x_ready"), 1)
                    if gain is not None and k >= 1:
                        h_low(p + 1, k - 1, gain)
                if gain is not None:
                    h_low(p + 1, DC - 1, gain)

            def rstd_kept(p):
                dve.wait_ge(sem("pre_root"), p + 1)
                rstd_rows()
                dve.wait_ge(sem("pre_spread"), p + 1)
                V.tensor_copy(ACC[:], PSF[:, 3072:3072 + T])
                fence().then_inc(sem("rstd_out"), 1)

            def ffn(l, f):
                n = l * 2 + f
                with dve.Fori(0, FT // 2) as i:
                    for jj in (0, 1):
                        j = i * 2 + jj
                        dve.wait_ge(sem("block_used0"), base(l, 0, 2 * f) + j + 1)
                        V.tensor_tensor(halves(SGB), pset(2 * jj), halves(ACC[:]), ALU.mult).then_inc(sem("gate_scaled"), 1)
                        dve.wait_ge(sem("block_used1"), base(l, 1, 2 * f) + j + 1)
                        V.tensor_tensor(halves(HB), pset(2 * jj + 1), halves(ACC[:]), ALU.mult).then_inc(sem("up_scaled"), 1)
                        fence()
                        dve.wait_ge(sem("silu"), 1 + n * FT + j)
                        V.tensor_tensor(HB, HB, SGB, ALU.mult)
                        fence().then_inc(sem("hidden"), 1)
                        dve.wait_ge(sem("hidden_hi"), n * FT + j + 1)
                        V.tensor_tensor(HID[:, j, 1, :], HB, HID[:, j, 0, :].bitcast(F32), ALU.subtract)
                        fence().then_inc(sem("hidden_split"), 1)

            V.memset(EPSC[:, 0:1], EPS)
            V.memset(EPSC[:, 1:2], 4 * EPS)
            V.memset(EPSC[:, 2:3], GN_EPS)
            fence().then_inc(sem("zeroed"), 1)
            for name in ("y_copied", "gate_scaled", "up_scaled"):
                dve.sem_inc(sem(name), 2)
            for name in ("y_added", "vec_ready"):
                dve.sem_inc(sem(name), 1)
            for i in range(TT):
                dve.wait_ge(sem("x_turned"), i + 1)
                V.tensor_copy(XT[:, :, i * P:(i + 1) * P], PSF[:, (i % 2) * 1024:(i % 2) * 1024 + 1024].rearrange("p (c n) -> p c n", c=DC))
                fence().then_inc(sem("x_placed"), 1)
            fence().then_inc(sem("x_ready"), DC)

            with dve.Fori(0, DEPTH) as l:
                dve.wait_ge(sem("vec_turned"), l + 1)
                V.tensor_copy(LV[:], PS[:, 6, 0:NV])
                fence()
                V.tensor_scalar(KA1[:], LV[:, VEC["k_a"][0]:VEC["k_a"][0] + GC], -1.0, 1.0, ALU.mult, ALU.add)
                fence().then_inc(sem("vec_ready"), 1)
                for k in range(DC):
                    h_low(l * 3, k, 0)
                rstd_kept(l * 3)
                ffn(l, 0)
                y_tiles(l * 3, lambda i, m: [((m * 3 + b) % 2, base(l, (m * 3 + b) % 2, 0) + FT + i * 3 + (m * 3 + b) // 2) for b in range(3)])
                norm_index = DC
                postnorm(l * 3)
                V.memset(RWP[:, :, 0:1], 0.0)
                V.memset(PBP[:, :, 0:POOL_ST], 0.0)
                V.memset(ZP[:, :, 0:2], 0.0)
                norm_index = 2 * DC
                prenorm(l * 3 + 1)
                V.memset(PW, 0.0)
                fence().then_inc(sem("poolw_zeroed"), 1)
                dve.wait_ge(sem("state_turned"), l + 1)
                ST7 = PS[:, 7, :]
                V.tensor_copy(RWS[:, :, :, 0], ST7[:, 0:RC * NSTR].rearrange("p (c b) -> p c b", c=RC))
                V.tensor_copy(ZS[:, :, :, 0:2], ST7[:, 64:96].rearrange("p (g b t) -> p g b t", g=GC, b=NSTR))
                V.tensor_copy(PBS[:, :, :, 0:POOL_ST], ST7[:, 128:368].rearrange("p (g b t) -> p g b t", g=GC, b=NSTR))
                fence().then_inc(sem("state_placed"), 1)
                for t in range(len(W_RWKV)):
                    c = W_RWKV[t] - GC
                    dve.wait_ge(sem("u_out"), 2 + l * NW + t + 1)
                    xp, xs = XS[:, c, 0:TP], XS[:, c, TP:T].rearrange("p (b t) -> p b t", b=NSTR)
                    V.tensor_tensor(xp, RWP[:, c, 0:TP], RWP[:, c, 1:1 + TP], ALU.subtract)
                    V.tensor_tensor(xs, RWS[:, c, :, 0:TS], RWS[:, c, :, 1:1 + TS], ALU.subtract)
                    fence()
                    V.scalar_tensor_tensor(out=xp, in0=xp, scalar=vec("mu", c), in1=RWP[:, c, 1:1 + TP], op0=ALU.mult, op1=ALU.add)
                    V.scalar_tensor_tensor(out=xs, in0=xs, scalar=vec("mu", c), in1=RWS[:, c, :, 1:1 + TS], op0=ALU.mult, op1=ALU.add)
                    if t == 0:
                        fence().then_inc(sem("ranks_shifted"), 1)
                    if t == 2:
                        fence()
                        for g in range(GC):
                            V.tensor_scalar(KK[:, g, :], XS[:, 2 + g, :], vec("k_k", g), None, ALU.mult)
                        fence()
                        V.tensor_tensor(SCR[:], KK[:], KK[:], ALU.mult)
                        fence().then_inc(sem("kk_squares"), 1)
                fence()
                R_, K_, V_ = XS[:, 0:2, :], XS[:, 2:4, :], XS[:, 4:6, :]
                dve.wait_ge(sem("tables_loaded"), (l + 1) * 3 * 16)
                dve.wait_ge(sem("decay_ready"), l + 1)
                for g in range(GC):
                    V.tensor_copy(CSP[:, g, :], CS[:, g, :])
                fence()
                for g in range(GC):
                    V.tensor_tensor_scan(CS[:, g, :], RESET[:], CSP[:, g, :], 0.0, ALU.mult, ALU.add)
                fence()
                V.tensor_tensor(CSP[:], CS[:], CSP[:], ALU.subtract)
                dve.wait_ge(sem("a_ready"), l + 1)
                for g in range(GC):
                    V.tensor_scalar(BV[:, g, :], BA[:, g, :], vec("k_a", g), KA1[:, g:g + 1], ALU.mult, ALU.add)
                fence()
                V.tensor_tensor(K_, K_, BV[:], ALU.mult)
                fence()
                for g in range(GC):
                    V.scalar_tensor_tensor(out=BV[:, g, :], in0=R_[:, g, :], scalar=vec("r_k", g), in1=K_[:, g, :], op0=ALU.mult, op1=ALU.mult)
                fence().then_inc(sem("bonus_in"), 1)
                dve.wait_ge(sem("kk_root"), l + 1)
                V.tensor_scalar(SCR[:], SCR[:], 1e-12, None, ALU.max)
                fence()
                V.reciprocal(SCR[:], SCR[:])
                fence()
                V.tensor_tensor(KK[:], KK[:], SCR[:], ALU.mult)
                fence()
                V.tensor_tensor(BA[:], BA[:], KK[:], ALU.mult)
                dve.wait_ge(sem("bonus_summed"), l + 1)
                V.tensor_tensor(BV[:].rearrange("p g (a n) -> p (g a) n", a=2), V_.rearrange("p g (a n) -> p (g a) n", a=2), PS[:, 4:8, 0:HALF], ALU.mult)
                fence()
                dve.wait_ge(sem("u_out"), 2 + l * NW + len(W_RWKV) + len(W_CONV))
                V.tensor_tensor(ZP[:, :, 2:], CV[:, 2:4, 0:TP], CV[:, 4:6, 0:TP], ALU.mult)
                for g in range(GC):
                    V.tensor_tensor(ZS[:, g, :, 2:], CV[:, 2 + g, TP:T].rearrange("p (b t) -> p b t", b=NSTR), CV[:, 4 + g, TP:T].rearrange("p (b t) -> p b t", b=NSTR), ALU.mult)
                fence()
                for g in range(GC):
                    yp, ys = CV[:, 2 + g, 0:TP], CV[:, 2 + g, TP:T].rearrange("p (b t) -> p b t", b=NSTR)
                    for w in range(CONV_W):
                        wv = vec("conv_w", w * GC + g)
                        zp, zs = ZP[:, g, w:w + TP], ZS[:, g, :, w:w + TS]
                        if w == 0:
                            V.tensor_scalar(yp, zp, wv, None, ALU.mult)
                            V.tensor_scalar(ys, zs, wv, None, ALU.mult)
                        else:
                            V.scalar_tensor_tensor(out=yp, in0=zp, scalar=wv, in1=yp, op0=ALU.mult, op1=ALU.add)
                            V.scalar_tensor_tensor(out=ys, in0=zs, scalar=wv, in1=ys, op0=ALU.mult, op1=ALU.add)
                        fence()
                V.tensor_tensor(CV[:, 4:6, :], CV[:, 2:4, :], CV[:, 0:2, :], ALU.mult)
                fence().then_inc(sem("conv_ready"), 1)
                dve.wait_ge(sem("u_out"), 2 + l * NW + len(W_RWKV) + len(W_CONV) + len(W_POOL))
                shift_t = TAIL[:, 0:63].rearrange("p (c n) -> p c n", c=RC)
                V.tensor_copy(shift_t[:, :, 0], RWP[:, :, TP])
                V.tensor_copy(shift_t[:, :, 1:9], RWS[:, :, :, TS])
                conv_t = TAIL[:, 64:100].rearrange("p (g n) -> p g n", g=GC)
                V.tensor_copy(conv_t[:, :, 0:2], ZP[:, :, TP:TP + 2])
                V.tensor_copy(conv_t[:, :, 2:18].rearrange("p g (b t) -> p g b t", b=NSTR), ZS[:, :, :, TS:TS + 2])
                V.tensor_copy(TAIL[:, 128:368].rearrange("p (g b t) -> p g b t", g=GC, b=NSTR), PBS[:, :, :, TS:TS + POOL_ST])
                V.tensor_copy(TAIL[:, 368:398].rearrange("p (g t) -> p g t", g=GC), PBP[:, :, TP:TP + POOL_ST])
                fence().then_inc(sem("tails_ready"), 1)
                NP, NSX = POOL_ST + TP, POOL_ST + TS
                DIF = CVF[:, 0:GC * T].rearrange("p (g t) -> p g t", g=GC)
                bufs = []
                for buf, at in ((CVF, GC * T), (OUTS, 1408 + G)):
                    bufs.append((buf[:, at:at + NP], buf[:, at + NP:at + NP + NSTR * NSX].rearrange("p (b t) -> p b t", b=NSTR)))
                for g in range(GC):
                    src = (PBP[:, g, :], PBS[:, g, :, :])
                    steps = ([(1, 0, 0), (2, 1, 64)] if g == 0 else [(1, 0, 0), (2, 1, 0), (4, 0, 0), (8, 1, 64)])
                    at = 0
                    for d, b, lo in steps:
                        at += d
                        V.tensor_tensor(bufs[b][0][lo:, at:], src[0][lo:, at:], src[0][lo:, at - d:NP - d], ALU.add)
                        V.tensor_tensor(bufs[b][1][lo:, :, at:], src[1][lo:, :, at:], src[1][lo:, :, at - d:NSX - d], ALU.add)
                        fence()
                        src = bufs[b]
                    for e in range(2):
                        pr = slice(64 * e, 64 * e + 64)
                        sp_, ss_ = bufs[e]
                        V.scalar_tensor_tensor(out=DIF[pr, g, 0:TP], in0=sp_[pr, POOL_ST:], scalar=IW[pr, g:g + 1], in1=PBP[pr, g, POOL_ST:], op0=ALU.mult, op1=ALU.subtract)
                        V.scalar_tensor_tensor(out=DIF[pr, g, TP:T].rearrange("p (b t) -> p b t", b=NSTR), in0=ss_[pr, :, POOL_ST:], scalar=IW[pr, g:g + 1], in1=PBS[pr, g, :, POOL_ST:], op0=ALU.mult, op1=ALU.subtract)
                    fence()
                    for e in range(2):
                        pr = slice(64 * e, 64 * e + 64)
                        V.tensor_tensor(DIF[pr, g, 0:16], bufs[e][0][pr, POOL_ST:POOL_ST + 16], ICNT[pr, g, :], ALU.mult)
                    fence()
                    V.tensor_tensor(DIF[:, g, 0:16], DIF[:, g, 0:16], PBP[:, g, POOL_ST:POOL_ST + 16], ALU.subtract)
                    fence()
                fence().then_inc(sem("pool_in"), 1)
                dve.wait_ge(sem("tails_turned"), l + 1)
                V.tensor_copy(OUTS[0:9, 0:RWKV_IN], PSF[0:9, 2048:2048 + RWKV_IN])
                V.tensor_copy(OUTS[0:18, 896:896 + G], PS[0:18, 6, 0:G])
                V.tensor_copy(OUTS[0:NSTR * POOL_ST, 1152:1152 + G], PS[0:NSTR * POOL_ST, 7, 0:G])
                V.tensor_copy(OUTS[0:POOL_ST, 1408:1408 + G], PS[0:POOL_ST, 7, G:2 * G])
                fence().then_inc(sem("tails_out"), 1)
                dve.wait_ge(sem("conv_hi"), l + 1)
                V.tensor_tensor(H[:, 4:6, 1, :], CV[:, 4:6, :], H[:, 4:6, 0, :].bitcast(F32), ALU.subtract)
                dve.wait_ge(sem("pool_hi"), l + 1)
                for g in range(GC):
                    V.scalar_tensor_tensor(out=halves(H[:, g, 1, :]), in0=pset(2 + g), scalar=vec("pool_scale", g), in1=halves(H[:, g, 0, :].bitcast(F32)), op0=ALU.mult, op1=ALU.subtract)
                fence()
                dve.wait_ge(sem("tails_stored"), (l + 1) * 6 * 16)
                V.memset(QM[:], 0.0)
                fence().then_inc(sem("attn_region"), 1)
                for g in range(GC):
                    V.tensor_copy(QM[:, g, :].rearrange("p (b n) -> p b n", b=NSTR)[:, :, 0:TS], SBQ[:, g, TP:T].rearrange("p (b t) -> p b t", b=NSTR))
                fence().then_inc(sem("qm_ready"), 1)
                for u in range(UNITS):
                    n = P * (u // NH + 1) if u < PT * NH else 2 * P
                    s = u % 2
                    dve.wait_ge(sem("sig_ready"), l * UNITS + u + 1)
                    ke = KE[:, s, :]
                    V.memset(ke[:, n:n + 1], 1.0)
                    V.tensor_tensor_scan(ke[:, n - 1::-1], ke[:, n - 1::-1], ke[:, n - 1::-1], 1.0, ALU.mult, ALU.bypass)
                    fence()
                    if u >= 2:
                        dve.wait_ge(sem("attn_turned"), l * UNITS + u - 1)
                    V.tensor_tensor(AW[:, s, 0:n], SIG[:, s, 0:n], ke[:, 1:n + 1], ALU.mult)
                    fence().then_inc(sem("attn_ready"), 1)

                def operands(tt):
                    ts = slice(tt * P, (tt + 1) * P)
                    dve.wait_ge(sem("exps_ready"), l * TT + tt + 1)
                    EP, EN, EPP = EXPS[:, 0], EXPS[:, 1], EXPS[:, 2]
                    per = TS if tt == PT else CH
                    n = P // per
                    AF, RF, PC = AFS[:, tt % 2], RFS[:, tt % 2], PCS[:, tt % 2]
                    V.tensor_tensor(BK[:, 0], EN, BA[:, :, ts], ALU.mult)
                    V.tensor_tensor(BK[:, 1], EN, K_[:, :, ts], ALU.mult)
                    V.tensor_tensor(AF, EPP, KK[:, :, ts], ALU.mult)
                    V.tensor_tensor(RF, EP, R_[:, :, ts], ALU.mult)
                    V.tensor_copy(PC[:, :, 0:n], EP.rearrange("p g (c n) -> p g c n", n=per)[:, :, :, per - 1])
                    fence()

                def placed_operands(tt):
                    per = TS if tt == PT else CH
                    n = P // per
                    AF, RF, PC = AFS[:, tt % 2], RFS[:, tt % 2], PCS[:, tt % 2]
                    for e in range(2):
                        pr = slice(64 * e, 64 * e + 64)
                        V.tensor_copy(AR[pr, e, :, 0, :], AF[pr])
                        V.tensor_copy(AR[pr, e, :, 1, :], RF[pr])
                    for k in range(2):
                        V.tensor_tensor(BP[:, k].rearrange("p g (c n) -> p g c n", n=per), BK[:, k].rearrange("p g (c n) -> p g c n", n=per),
                                        PC[:, :, 0:n].unsqueeze(3).broadcast_to([P, GC, n, per]), ALU.mult)
                    fence().then_inc(sem("operands"), 1)

                dve.wait_ge(sem("attn_done"), (l + 1) * UNITS)
                dve.wait_ge(sem("kv_stored"), (l + 1) * 4 * 16)
                V.memset(AR[:], 0.0)
                fence().then_inc(sem("attn_over"), 1)
                operands(0)
                placed_operands(0)
                dve.wait_ge(sem("attn_hi"), l + 1)
                V.tensor_tensor(H[:, 6:8, 1, 0:TP], PS[:, 4:6, :], H[:, 6:8, 0, 0:TP].bitcast(F32), ALU.subtract)
                V.tensor_tensor(H[:, 6:8, 1, TP:T], PS[:, 6:8, 0:P], H[:, 6:8, 0, TP:T].bitcast(F32), ALU.subtract)
                fence().then_inc(sem("attn_split"), 1)
                V.memset(ST[:], 0.0)
                V.memset(RH[:], 0.0)
                V.memset(NU[:], 0.0)
                V.memset(SN.rearrange("p b g n -> p (b g n)"), 0.0)
                fence().then_inc(sem("states_zeroed"), 1)
                dve.wait_ge(sem("masks_loaded"), (l + 1) * 4 * 16)
                for tt in range(TT):
                    q = l * TT + tt
                    sample = tt == PT
                    ts = slice(tt * P, (tt + 1) * P)
                    AF, RF, PC = AFS[:, tt % 2], RFS[:, tt % 2], PCS[:, tt % 2]
                    nlev = SAMPLE_LEVELS if sample else PROMPT_LEVELS
                    lev0, inner0 = levels_before(l, tt), inner_levels_before(l, tt)
                    dve.wait_ge(sem("scores_in"), q + 1)
                    if sample:
                        dve.wait_ge(sem("sample_tri_loaded"), (l + 1) * 16)
                    tri = TRI[:].rearrange("p a n -> p (a n)").unsqueeze(1).broadcast_to([P, NH, 2 * P])

                    def by_head(ap):
                        return ap.rearrange("p (h n) -> p h n", n=P)

                    def every_head(ap, n=NH):
                        return ap.unsqueeze(1).broadcast_to([P, n, P])

                    beta_scores = PSF[:, 0:1024].rearrange("p (h a n) -> p h a n", h=NH, a=2)
                    V.tensor_tensor(LTG[:, :, 0, :], beta_scores[:, :, 0, :], every_head(TRI[:, 0, :]), ALU.mult)
                    V.tensor_tensor(X[:], by_head(PS[:, 4, :]), every_head(LEV1[:]), ALU.mult)
                    fence().then_inc(sem("lt_ready"), 1)
                    V.tensor_tensor(NT[:, 0], LTG[:, :, 0, :], every_head(LEV[:, 1, :]), ALU.mult)
                    fence()
                    for a in (0, 1):
                        hs = slice(2 * a, 2 * a + 2)
                        V.tensor_tensor(X[:, hs], every_head(IDENT, 2), X[:, hs], ALU.subtract).then_inc(sem(f"x_ready{a}"), 1)
                    V.tensor_tensor(XTR[:], LTG[:, :, 0, :], every_head(LEV[:, 0, :]), ALU.mult)
                    fence()
                    for a in (0, 1):
                        hs = slice(2 * a, 2 * a + 2)
                        V.tensor_tensor(XTR[:, hs], every_head(IDENT, 2), XTR[:, hs], ALU.subtract).then_inc(sem(f"xt_ready{a}"), 1)
                    V.tensor_tensor(LTG[:, :, 1, :], beta_scores[:, :, 1, :], every_head(TRI[:, 1, :]), ALU.mult)
                    dve.wait_ge(sem("kappa_scores_in"), q + 1)
                    V.tensor_tensor(KTG[:].rearrange("p h a n -> p h (a n)"), PSF[:, 1024:2048].rearrange("p (h n) -> p h n", h=NH), tri, ALU.mult)
                    fence().then_inc(sem("scores_masked"), 1)
                    for v in range(nlev):
                        for a in (0, 1):
                            hs = slice(2 * a, 2 * a + 2)
                            if v + 1 < nlev:
                                dve.wait_ge(sem(f"x_update_in{a}"), inner0 + v + 1)
                                V.tensor_tensor(X[:, hs], X[:, hs], by_head(PS[:, 4 + 2 * a, 256:512]), ALU.subtract).then_inc(sem(f"x_ready{a}"), 1)
                            dve.wait_ge(sem(f"xt_update_in{a}"), lev0 + v + 1)
                            V.tensor_tensor(XTR[:, hs], XTR[:, hs], by_head(PS[:, 5 + 2 * a, 0:256]), ALU.subtract).then_inc(sem(f"xt_ready{a}"), 1)
                        if v == 1:
                            dve.wait_ge(sem("mv_in"), q + 1)
                            V.tensor_copy(MVS[:], PS[:, 0, G:2 * G])
                        if v == 2 and not sample:
                            operands(tt + 1)
                        if v == 3 and not sample:
                            placed_operands(tt + 1)
                    fence()
                    if not sample:
                        for c in range(NCH):
                            r = slice(64 * c, 64 * c + 64)
                            dve.wait_ge(sem("rhs_in"), l * (PT * NCH + 1) + tt * NCH + c + 1)
                            V.tensor_tensor(RH[r, :], PS[r, 0, 0:G], MVS[r, :], ALU.add).then_inc(sem("rhs_ready"), 1)
                            dve.wait_ge(sem("state_in"), l * PT * NCH + tt * NCH + c + 1)
                            for g in range(GC):
                                for e in range(2):
                                    pr = slice(64 * e, 64 * e + 64)
                                    V.scalar_tensor_tensor(out=ST[pr, g, pr], in0=ST[pr, g, pr], scalar=PC[pr, g, c:c + 1],
                                                           in1=PS[pr, 4, g * P + 64 * e:g * P + 64 * e + 64], op0=ALU.mult, op1=ALU.add)
                            fence().then_inc(sem("state_ready"), 1)
                    else:
                        dve.wait_ge(sem("rhs_in"), l * (PT * NCH + 1) + PT * NCH + 1)
                        V.tensor_tensor(RH[:], PS[:, 0, 0:G], MVS[:], ALU.add).then_inc(sem("rhs_ready"), 1)

                        def head_states(h):
                            pr = slice(64 * (h % 2), 64 * (h % 2) + 64)
                            return pr, h // 2, STS[pr, :, h // 2, pr]

                        def spread_u(h):
                            if h >= 2:
                                dve.wait_ge(sem("sample_delta"), l * NH + h - 1)
                            V.tensor_tensor(by_stream(NMU[h % 2]), NU[:, h * HD:(h + 1) * HD].unsqueeze(1).broadcast_to([P, NSTR, HD]),
                                            ROWM[:].unsqueeze(2).broadcast_to([P, NSTR, HD]), ALU.mult).then_inc(sem("spread_u"), 1)

                        for h in range(NH):
                            pr, g, sv = head_states(h)
                            V.tensor_tensor(sv, sv, PC[pr, g, :].unsqueeze(2).broadcast_to([64, NSTR, HD]), ALU.mult)
                        fence()
                        dve.wait_ge(sem("u_done"), l * (PT * NCH + 1) + PT * NCH + 1)
                        spread_u(0)
                        for h in range(NH):
                            if h + 1 < NH:
                                spread_u(h + 1)
                            pr, g, sv = head_states(h)
                            dve.wait_ge(sem("sample_delta"), l * NH + h + 1)
                            V.tensor_tensor(sv, sv, by_stream(PS[pr, 4 + h, :]), ALU.add)
                        fence().then_inc(sem("sample_states"), 1)
                    fence()
                dve.wait_ge(sem("mean_in"), l + 1)
                flat = lambda a: a.rearrange("p g (a n) -> p (g a) n", a=2)
                V.scalar_tensor_tensor(out=flat(CSP[:]), in0=PS[:, 0:4, 0:HALF], scalar=-1.0 / HD, in1=flat(CSP[:]), op0=ALU.mult, op1=ALU.add)
                fence()
                V.tensor_tensor(SCR[:], CSP[:], CSP[:], ALU.mult)
                fence().then_inc(sem("centred"), 1)
                dve.wait_ge(sem("var_root"), l + 1)
                V.reciprocal(HCOLS[:], HCOLS[:])
                fence()
                V.tensor_copy(TAIL[:, 0:TT * G].rearrange("p (i n) -> p i n", n=HD), HCOLS[:].unsqueeze(2).broadcast_to([P, TT * NH, HD]))
                fence().then_inc(sem("inverse_rows"), 1)
                dve.wait_ge(sem("inverse_spread"), l + 1)
                for g in range(GC):
                    V.tensor_tensor(SCR[:, g, :], PSF[:, 2048 + g * 1024:2048 + g * 1024 + T], CSP[:, g, :], ALU.mult)
                fence()
                for g in range(GC):
                    V.tensor_scalar(SCR[:, g, :], SCR[:, g, :], vec("ln_w", g), vec("ln_b", g), ALU.mult, ALU.add)
                fence()
                V.tensor_tensor(SCR[:], SCR[:], BV[:], ALU.add)
                fence()
                V.tensor_tensor(SCR[:], SCR[:], GA[:], ALU.mult)
                fence().then_inc(sem("yr_ready"), 1)
                dve.wait_ge(sem("yr_hi"), l + 1)
                V.tensor_tensor(H[:, 2:4, 1, :], SCR[:], H[:, 2:4, 0, :].bitcast(F32), ALU.subtract)
                fence().then_inc(sem("mixed"), 1)
                dve.wait_ge(sem("wkv_stored"), (l + 1) * 8 * 16)
                y_tiles(l * 3 + 1, lambda i, m: [(m, base(l, m, 1) + ((NW + 1) // 2, NW // 2)[m] + i)], YM)
                norm_index = 3 * DC
                postnorm(l * 3 + 1, YM, 4 * DC)
                rstd_kept(l * 3 + 2)
                ffn(l, 1)
                y_tiles(l * 3 + 2, lambda i, m: [((m * 3 + b) % 2, base(l, (m * 3 + b) % 2, 2) + FT + i * 3 + (m * 3 + b) // 2) for b in range(3)])
                norm_index = 5 * DC
                postnorm(l * 3 + 2)

        @block.tensor
        def _(pe):
            MM = nc.tensor.matmul

            def turn(out, in_):
                return nc.tensor.transpose(out, in_, IDENT[0:in_.shape[0], 0:in_.shape[0]])

            def split_product(q, s, slot, mov, first, last):
                hi, lo = WSP[s][:, 0, slot, :], WSP[s][:, 1, slot, :]
                for a in (0, 1):
                    out = PS[:, 2 * q + a, 0:HALF]
                    cols = slice(a * HALF, (a + 1) * HALF)
                    MM(out, hi, mov[:, 0, cols], start=first, stop=False)
                    MM(out, hi, mov[:, 1, cols], start=False, stop=False)
                    end = MM(out, lo, mov[:, 0, cols], start=False, stop=last)
                return end

            def token_sums(src):
                for i in range(TT):
                    end = MM(PS[:, 7, i:i + 1], src[:, i * P:(i + 1) * P], ONES[:, 0:1], start=True, stop=True)
                return end

            def spread(bank):
                MM(PS[:, bank, :], ONES, ACC[:, 0:512], start=True, stop=True)
                return MM(PS[:, bank + 1, 0:P], ONES, ACC[:, 512:T], start=True, stop=True)

            def square_sums(p):
                pe.wait_ge(sem("squares_summed"), (p + 1) * (DC - 1))
                token_sums(ACC[:]).then_inc(sem("pre_summed"), 1)

            def prenorm(p):
                square_sums(p)
                pe.wait_ge(sem("diagonals"), 2 * p + 1)
                spread(4).then_inc(sem("pre_spread"), 1)

            def postnorm(p):
                pe.wait_ge(sem("y_added"), 1 + (p + 1) * DC)
                token_sums(ACC[:]).then_inc(sem("post_summed"), 1)
                pe.wait_ge(sem("diagonals"), 2 * p + 2)
                spread(4).then_inc(sem("post_spread"), 1)

            def from_h(q, s, k, p, wait_h):
                pe.wait_ge(sem(f"lo_ready{s}"), k + 2)
                for c in range(DC):
                    if wait_h:
                        pe.wait_ge(sem("h_ready"), p * DC + c + 1)
                    end = split_product(q, s, c, H[:, c], c == 0, c == DC - 1)
                end.then_inc(sem(f"block_used{s}"), 1)

            def ffn(l, f):
                n, p = l * 2 + f, l * 3 + 2 * f
                for s in (0, 1):
                    pe.wait_ge(sem(f"lo_ready{s}"), base(l, s, 2 * f) + 2)
                if f == 0:
                    pe.wait_ge(sem("vec_loaded"), (l + 1) * len(VEC) * 16)
                    turn(PS[:, 6, 0:NV], VROW[:]).then_inc(sem("vec_turned"), 1)
                for k in range(DC):
                    c = DC - 1 - k
                    pe.wait_ge(sem("h_ready"), p * DC + k + 1)
                    end = split_product(0, 0, c, H[:, c], k == 0, k == DC - 1)
                    if k % 2:
                        split_product(1, 1, DC - 1 - k // 2, H[:, DC - 1 - k // 2], k == 1, False)
                end.then_inc(sem("block_used0"), 1)
                square_sums(p)
                for c in reversed(range(DC // 2)):
                    end = split_product(1, 1, c, H[:, c], False, c == 0)
                end.then_inc(sem("block_used1"), 1)
                pe.wait_ge(sem("diagonals"), 2 * p + 1)
                spread(6).then_inc(sem("pre_spread"), 1)
                from_h(2, 0, base(l, 0, 2 * f) + 1, p, False)
                pe.wait_ge(sem("rstd_out"), n + 1)
                from_h(3, 1, base(l, 1, 2 * f) + 1, p, False)
                with pe.Fori(1, FT // 2) as i:
                    for jj in (0, 1):
                        j = i * 2 + jj
                        pe.wait_ge(sem("gate_scaled"), 1 + n * FT + j)
                        from_h(2 * jj, 0, base(l, 0, 2 * f) + j, p, False)
                        pe.wait_ge(sem("up_scaled"), 1 + n * FT + j)
                        from_h(2 * jj + 1, 1, base(l, 1, 2 * f) + j, p, False)
                with pe.Fori(0, DC // 2) as i:
                    for m in (0, 1):
                        pe.wait_ge(sem("y_copied"), 1 + p * DC + i * 2 + m)
                        pe.wait_ge(sem("up_scaled"), 2 + n * FT + FT)
                        for b, (r0, r1) in enumerate(DOWN_CUTS):
                            s = (m * 3 + b) % 2
                            pe.wait_ge(sem(f"lo_ready{s}"), base(l, s, 2 * f) + FT + i * 3 + (m * 3 + b) // 2 + 2)
                            if m == 0:
                                pe.wait_ge(sem("hidden_split"), n * FT + r1)
                            for r in range(r0, r1):
                                end = split_product(m, s, r - r0, HID[:, r], r == 0, r == FT - 1)
                            end.then_inc(sem(f"block_used{s}"), 1)
                postnorm(p)

            pe.wait_ge(sem("consts_loaded"), 16)
            for i in range(TT):
                pe.wait_ge(sem(f"x_loaded{i}"), 16)
                if i >= 2:
                    pe.wait_ge(sem("x_placed"), i - 1)
                for c in range(DC):
                    at = (i % 2) * 1024 + c * P
                    end = turn(PSF[:, at:at + P], IO[:, i, c * P:(c + 1) * P])
                end.then_inc(sem("x_turned"), 1)
            with pe.Fori(0, DEPTH) as l:
                ffn(l, 0)
                prenorm(l * 3 + 1)
                def rank_product(lo, hi):
                    for o in range(GC):
                        for a in (0, 1):
                            end = MM(PS[:, 2 * (2 + o) + a, 0:HALF], SMALLW[lo:hi, o * P:(o + 1) * P], XS[lo:hi, 6, a * HALF:(a + 1) * HALF], start=True, stop=True)
                    return end

                def head_sums(src, q):
                    for g in range(GC):
                        for a in (0, 1):
                            end = MM(PS[:, 2 * (q + g) + a, 0:HALF], HEADS, src[:, g, a * HALF:(a + 1) * HALF], start=True, stop=True)
                    return end

                for t in range(NW):
                    pe.wait_ge(sem("u_out"), 1 + l * NW + t)
                    from_h(t % 2, t % 2, base(l, t % 2, 1) + t // 2, l * 3 + 1, t == 0)
                    if t == STATES_AT:
                        pe.wait_ge(sem("state_loaded"), (l + 1) * 3 * 16)
                        for g in range(GC):
                            turn(PS[:, 7, 128 + 120 * g:248 + 120 * g], STIN2[0:120, G + g * P:G + (g + 1) * P])
                        for g in range(GC):
                            turn(PS[:, 7, 64 + 16 * g:80 + 16 * g], STIN2[0:16, g * P:(g + 1) * P])
                        for c in range(RC):
                            end = turn(PS[:, 7, c * NSTR:(c + 1) * NSTR], STIN[0:NSTR, c * P:(c + 1) * P])
                        end.then_inc(sem("state_turned"), 1)
                    if t == DECAY_AT:
                        pe.wait_ge(sem("rank_loaded"), (l + 1) * 3 * 16)
                        pe.wait_ge(sem("gates_ready"), l + 1)
                        pe.wait_ge(sem("state_placed"), l + 1)
                        rank_product(0, 32).then_inc(sem("decay_in"), 1)
                    if t == A_AT:
                        pe.wait_ge(sem("decay_ready"), l + 1)
                        rank_product(32, 64).then_inc(sem("a_in"), 1)
                    if t == GATE_AT:
                        pe.wait_ge(sem("a_ready"), l + 1)
                        rank_product(64, 128).then_inc(sem("gate_in"), 1)
                    if t == KK_AT:
                        pe.wait_ge(sem("kk_squares"), l + 1)
                        pe.wait_ge(sem("gate_ready"), l + 1)
                        head_sums(SCR, 2).then_inc(sem("kk_summed"), 1)
                    if t == BONUS_AT:
                        pe.wait_ge(sem("kk_root"), l + 1)
                        pe.wait_ge(sem("bonus_in"), l + 1)
                        head_sums(BV, 2).then_inc(sem("bonus_summed"), 1)
                    if t == TAILS_AT:
                        pe.wait_ge(sem("tails_ready"), l + 1)
                        for c in range(RC):
                            turn(PSF[0:9, 2048 + c * P:2048 + (c + 1) * P], TAIL[:, c * 9:(c + 1) * 9])
                        for g in range(GC):
                            turn(PS[0:18, 6, g * P:(g + 1) * P], TAIL[:, 64 + 18 * g:82 + 18 * g])
                        for g in range(GC):
                            turn(PS[0:120, 7, g * P:(g + 1) * P], TAIL[:, 128 + 120 * g:248 + 120 * g])
                        for g in range(GC):
                            end = turn(PS[0:15, 7, G + g * P:G + (g + 1) * P], TAIL[:, 368 + 15 * g:383 + 15 * g])
                        end.then_inc(sem("tails_turned"), 1)
                pe.wait_ge(sem("poolw_loaded"), (l + 1) * 4 * 16)
                pe.wait_ge(sem("tails_out"), l + 1)
                pe.wait_ge(sem("pool_in"), l + 1)
                for g in range(GC):
                    for a in (0, 1):
                        end = MM(PS[:, 2 * (2 + g) + a, 0:HALF], PW[:, g, :], CVF[:, g * T + a * HALF:g * T + (a + 1) * HALF], start=True, stop=True)
                end.then_inc(sem("pool_out"), 1)

                pe.wait_ge(sem("attn_region"), l + 1)
                for i in range(TT):
                    if i >= 2:
                        pe.wait_ge(sem("kv_out"), l * TT + i - 1)
                    for c in range(4):
                        end = turn(PS[:, i % 2, c * P:(c + 1) * P], SBQ[:, 2 + c, i * P:(i + 1) * P])
                    end.then_inc(sem("kv_turned"), 1)
                pe.wait_ge(sem("kc_loaded"), (l + 1) * 16)
                for g in range(GC):
                    for b in range(NSTR):
                        at = 1024 + (g * NSTR + b) * P
                        end = turn(PSF[:, at:at + P], KC[:, b, g * P:(g + 1) * P])
                end.then_inc(sem("kc_turned"), 1)

                def scores(u):
                    i, h = u // NH, u % NH
                    pr, g = slice(64 * (h % 2), 64 * (h % 2) + 64), h // 2
                    if u >= 2:
                        pe.wait_ge(sem("sig_ready"), l * UNITS + u - 1)
                    z = PS[:, u % 2, :]
                    if i < PT:
                        n = (i + 1) * P
                        MM(z[:, n - P:n], IDENT, SEE[0], start=True, stop=False, skip_group_check=True)
                        end = MM(z[:, 0:n], SBQ[pr, g, i * P:(i + 1) * P], SBQ[pr, 2 + g, 0:n], start=False, stop=True, skip_group_check=True)
                    else:
                        n = 2 * P
                        MM(z[:, PAST:n], IDENT, SEE[1], start=True, stop=False, skip_group_check=True)
                        MM(z[:, PAST:n], SBQ[pr, g, TP:T], SBQ[pr, 2 + g, TP:T], start=False, stop=True, skip_group_check=True)
                        for b in range(NSTR):
                            end = MM(z[:, 0:PAST], QM[pr, g, b * P:(b + 1) * P], KCT[pr, g, b, :], start=False, stop=b == NSTR - 1, skip_group_check=True)
                    end.then_inc(sem("z_ready"), 1)

                def turn_attn(u):
                    nb = (u // NH + 1) if u < PT * NH else 2
                    pe.wait_ge(sem("attn_ready"), l * UNITS + u + 1)
                    if u >= 2:
                        pe.wait_ge(sem("attnT_out"), l * UNITS + u - 1)
                    for b in range(nb):
                        end = turn(PS[:, 2 + u % 2, b * P:(b + 1) * P], AW[:, u % 2, b * P:(b + 1) * P])
                    end.then_inc(sem("attn_turned"), 1)

                def values(u):
                    i, h = u // NH, u % NH
                    pr, g = slice(64 * (h % 2), 64 * (h % 2) + 64), h // 2
                    hc = slice(h * HD, (h + 1) * HD)
                    pe.wait_ge(sem("attnT_out"), l * UNITS + u + 1)
                    if i < PT:
                        for b in range(i + 1):
                            end = MM(PS[pr, 4 + g, i * P:(i + 1) * P], VT[:, b, hc], AT[:, u % 2, b, :], start=b == 0, stop=b == i)
                    else:
                        MM(PS[pr, 6 + g, 0:P], VT[:, PT, hc], AT[:, u % 2, 1, :], start=True, stop=False, skip_group_check=True)
                        for b in range(NSTR):
                            end = MM(PS[pr, 6 + g, b * TS:(b + 1) * TS], VC[:, b, hc], AT[:, u % 2, 0, b * TS:(b + 1) * TS], start=False, stop=b == NSTR - 1, skip_group_check=True)
                    end.then_inc(sem("attn_done"), 1)

                pe.wait_ge(sem("kcT_out"), l + 1)
                pe.wait_ge(sem("kv_out"), (l + 1) * TT)
                pe.wait_ge(sem("pool_hi"), l + 1)
                pe.wait_ge(sem("qm_ready"), l + 1)
                pe.wait_ge(sem("vc_loaded"), (l + 1) * 16)
                for u in range(UNITS + 2):
                    if u < UNITS:
                        scores(u)
                    if 1 <= u <= UNITS:
                        turn_attn(u - 1)
                    if u >= 2:
                        values(u - 2)

                pe.wait_ge(sem("attn_split"), l + 1)

                def heads():
                    for h in range(NH):
                        yield h, h // 2, h % 2, slice(h * HD, (h + 1) * HD), slice(64 * (h % 2), 64 * (h % 2) + 64)

                for tt in range(TT):
                    q = l * TT + tt
                    sample = tt == PT
                    ts = slice(tt * P, (tt + 1) * P)
                    nlev = SAMPLE_LEVELS if sample else PROMPT_LEVELS
                    lev0, inner0 = levels_before(l, tt), inner_levels_before(l, tt)
                    AF, RF = AFS[:, tt % 2], RFS[:, tt % 2]
                    pe.wait_ge(sem("operands"), q + 1)
                    for k in range(2):
                        for g in range(GC):
                            turn(PS[:, 5, (2 * k + g) * P:(2 * k + g + 1) * P], BP[:, k, g, :])
                    for g in range(GC):
                        turn(PS[:, 6, g * P:(g + 1) * P], XS[:, 4 + g, ts])
                    for h, g, e, hc, pr in heads():
                        MM(PSF[:, h * 256:h * 256 + 256], BK[:, 0, g, :], AR[:, e, g, :, :].rearrange("p a n -> p (a n)"), start=True, stop=True)
                    if sample:
                        pe.wait_ge(sem("prompt_state_out"), l + 1)
                    elif tt:
                        pe.wait_ge(sem("state_ready"), l * PT * NCH + tt * NCH)
                    for h, g, e, hc, pr in heads():
                        end = MM(PS[:, 4, h * P:(h + 1) * P], AR[:, e, g, 0, :], BK[:, 0, g, :], start=True, stop=True)
                    end.then_inc(sem("scores_in"), 1)
                    if tt:
                        pe.wait_ge(sem("yr_out"), q)
                    for h, g, e, hc, pr in heads():
                        end = MM(PSF[:, 1024 + h * 256:1280 + h * 256], BK[:, 1, g, :], AR[:, e, g, :, :].rearrange("p a n -> p (a n)"), start=True, stop=True)
                    end.then_inc(sem("kappa_scores_in"), 1)
                    if tt == 0:
                        pe.wait_ge(sem("states_zeroed"), l + 1)
                    pe.wait_ge(sem("rows_ready"), q + 1)
                    for v in range(nlev):
                        if v:
                            pe.wait_ge(sem("blocks_ready"), inner0 + v)
                        for a in (0, 1):
                            pe.wait_ge(sem(f"x_ready{a}"), lev0 + v + 1)
                            for h in (2 * a, 2 * a + 1):
                                end = MM(PS[:, 4 + 2 * a, (h % 2) * P:(h % 2 + 1) * P], NT[:, v % 2, h, :], X[:, h, :], start=True, stop=True)
                            end.then_inc(sem(f"t1_in{a}"), 1)
                        if v == 1:
                            pe.wait_ge(sem("scores_masked"), q + 1)
                            for h, g, e, hc, pr in heads():
                                end = MM(PS[:, 0, G + h * HD:G + (h + 1) * HD], KTG[:, h, 0, :], TOK[:, 2, hc], start=True, stop=True)
                            end.then_inc(sem("mv_in"), 1)
                            if not sample:
                                for h, g, e, hc, pr in heads():
                                    MM(PS[pr, 2 + g, 0:P], TOK[:, 2, hc], KTG[:, h, 1, :], start=True, stop=False, skip_group_check=True)
                        for a in (0, 1):
                            pe.wait_ge(sem(f"t1_out{a}"), lev0 + v + 1)
                            pe.wait_ge(sem(f"xt_ready{a}"), lev0 + q + v + 1)
                            if v + 1 < nlev:
                                for h in (2 * a, 2 * a + 1):
                                    end = MM(PS[:, 4 + 2 * a, 256 + (h % 2) * P:256 + (h % 2 + 1) * P], XTR[:, h, :], T1[:, h, :], start=True, stop=True)
                                end.then_inc(sem(f"x_update_in{a}"), 1)
                            for h in (2 * a, 2 * a + 1):
                                end = MM(PS[:, 5 + 2 * a, (h % 2) * P:(h % 2 + 1) * P], T1[:, h, :], XTR[:, h, :], start=True, stop=True)
                            end.then_inc(sem(f"xt_update_in{a}"), 1)
                    for a in (0, 1):
                        pe.wait_ge(sem(f"xt_ready{a}"), lev0 + q + nlev + 1)
                    if not sample:
                        for c in range(NCH):
                            r, n = slice(64 * c, 64 * c + 64), tt * NCH + c
                            if n:
                                pe.wait_ge(sem("state_ready"), l * PT * NCH + n)
                            for g in range(GC):
                                end = MM(PS[r, 0, g * P:(g + 1) * P], AF[:, g, r], ST[:, g, :], start=True, stop=True)
                            end.then_inc(sem("rhs_in"), 1)
                            for g in range(GC):
                                MM(PS[:, 2 + g, r], ST[:, g, :], RF[:, g, r], start=False, stop=False, skip_group_check=True)
                            for g in range(GC):
                                gc = slice(g * P, (g + 1) * P)
                                MM(PS[:, 4, gc], TOK[r, 1, gc], TOK[r, 2, gc], start=g == 0, stop=False, skip_group_check=True)
                            pe.wait_ge(sem("rhs_ready"), l * (PT * NCH + 1) + n + 1)
                            for h, g, e, hc, pr in heads():
                                end = MM(PS[r, 1, hc], XTR[:, h, r], RH[:, hc], start=True, stop=True)
                            end.then_inc(sem("u_in"), 1)
                            pe.wait_ge(sem("u_done"), l * (PT * NCH + 1) + n + 1)
                            for g in range(GC):
                                gc = slice(g * P, (g + 1) * P)
                                end = MM(PS[:, 4, gc], TOK[r, 0, gc], NU[r, gc], start=False, stop=True, skip_group_check=True)
                            end.then_inc(sem("state_in"), 1)
                            for h, g, e, hc, pr in heads():
                                end = MM(PS[pr, 2 + g, r], NU[:, hc], LTG[:, h, 1, r], start=False, stop=True, skip_group_check=True)
                        end.then_inc(sem("yr_in"), 1)
                        if tt == PT - 1:
                            pe.wait_ge(sem("state_ready"), (l + 1) * PT * NCH)
                            for g in range(GC):
                                end = turn(PS[:, 4, g * P:(g + 1) * P], ST[:, g, :])
                            end.then_inc(sem("prompt_state_in"), 1)
                    else:
                        pe.wait_ge(sem("wkv_loaded"), (l + 1) * 4 * 16)
                        for b in range(NSTR):
                            for g in range(GC):
                                at = (b * GC + g) * P
                                end = turn(PSF[:, at:at + P], SN[:, b, g, :])
                        end.then_inc(sem("stateT_in"), 1)
                        pe.wait_ge(sem("stateT_out"), l + 1)
                        for h, g, e, hc, pr in heads():
                            MM(PS[pr, 2 + g, 0:P], TOK[:, 2, hc], KTG[:, h, 1, :], start=True, stop=False, skip_group_check=True)
                        for b in range(NSTR):
                            for g in range(GC):
                                cs = slice(g * P + b * TS, g * P + (b + 1) * TS)
                                end = MM(PS[:, 4, cs], STS[:, b, g, :], AF[:, g, b * TS:(b + 1) * TS], start=True, stop=True)
                        end.then_inc(sem("state_rhs_in"), 1)
                        for b in range(NSTR):
                            for g in range(GC):
                                MM(PS[:, 2 + g, b * TS:(b + 1) * TS], STS[:, b, g, :], RF[:, g, b * TS:(b + 1) * TS], start=False, stop=False, skip_group_check=True)
                        pe.wait_ge(sem("state_rhs_out"), l + 1)
                        T1F = T1[:].rearrange("p h n -> p (h n)")
                        for g in range(GC):
                            end = turn(PS[:, 0, g * P:(g + 1) * P], T1F[:, g * P:(g + 1) * P])
                        end.then_inc(sem("rhs_in"), 1)
                        pe.wait_ge(sem("rhs_ready"), l * (PT * NCH + 1) + PT * NCH + 1)
                        for h, g, e, hc, pr in heads():
                            end = MM(PS[:, 1, hc], XTR[:, h, :], RH[:, hc], start=True, stop=True)
                        end.then_inc(sem("u_in"), 1)
                        pe.wait_ge(sem("u_done"), l * (PT * NCH + 1) + PT * NCH + 1)
                        for h, g, e, hc, pr in heads():
                            end = MM(PS[pr, 2 + g, 0:P], NU[:, hc], LTG[:, h, 1, :], start=False, stop=True, skip_group_check=True)
                        end.then_inc(sem("yr_in"), 1)
                        for h, g, e, hc, pr in heads():
                            gc = slice(g * P, (g + 1) * P)
                            pe.wait_ge(sem("spread_u"), l * NH + h + 1)
                            MM(PS[:, 4 + h, :], TOK[:, 0, gc], NMU[h % 2], start=True, stop=False)
                            pe.wait_ge(sem("kappa_spread"), l * NH + h + 1)
                            MM(PS[:, 4 + h, :], TOK[:, 1, gc], NMK[h % 2], start=False, stop=True).then_inc(sem("sample_delta"), 1)
                        pe.wait_ge(sem("sample_states"), l + 1)
                        pe.wait_ge(sem("yr_out"), q + 1)
                        for b in range(NSTR):
                            for g in range(GC):
                                at = (b * GC + g) * P
                                end = turn(PSF[:, at:at + P], STS[:, b, g, :])
                        end.then_inc(sem("sample_state_in"), 1)
                pe.wait_ge(sem("sample_state_out"), l + 1)
                head_sums(CSP, 0).then_inc(sem("mean_in"), 1)
                pe.wait_ge(sem("centred"), l + 1)
                for i in range(TT):
                    for g in range(GC):
                        at = i * NH + g * 2
                        end = MM(PS[:, 4, at:at + 2], SCR[:, g, i * P:(i + 1) * P], HEADS[:, 0:P:HD], start=True, stop=True)
                end.then_inc(sem("var_in"), 1)

                kb = ((NW + 1) // 2, NW // 2)
                rule_rows = (2, 3)
                for m in (0, 1):
                    pe.wait_ge(sem(f"lo_ready{m}"), base(l, m, 1) + kb[m] + 2)
                    for c in range(DC):
                        if c not in rule_rows:
                            split_product(m, m, c, H[:, c], c == 0, False)
                    if m == 0:
                        pe.wait_ge(sem("inverse_rows"), l + 1)
                        for g in range(GC):
                            for i in range(TT):
                                at = 2048 + g * 1024 + i * P
                                end = turn(PSF[:, at:at + P], TAIL[:, i * G + g * P:i * G + (g + 1) * P])
                        end.then_inc(sem("inverse_spread"), 1)
                pe.wait_ge(sem("mixed"), l + 1)
                for m in (0, 1):
                    for c in rule_rows:
                        end = split_product(m, m, c, H[:, c], False, c == rule_rows[-1])
                    end.then_inc(sem(f"block_used{m}"), 1)
                with pe.Fori(1, DC // 2) as i:
                    for m in (0, 1):
                        pe.wait_ge(sem("y_copied"), 1 + (l * 3 + 1) * DC + i * 2 + m)
                        from_h(m, m, base(l, m, 1) + kb[m] + i, l * 3 + 1, False)
                postnorm(l * 3 + 1)
                ffn(l, 1)
            pe.wait_ge(sem("x_ready"), (DEPTH * 3 + 1) * DC)
            for i in range(TT):
                if i >= 2:
                    pe.wait_ge(sem("out_rows"), i - 1)
                for c in range(DC):
                    at = (i % 2) * 1024 + c * P
                    end = turn(PSF[:, at:at + P], XT[:, c, i * P:(i + 1) * P])
                end.then_inc(sem("rows_in"), 1)


_INS = ["x_prompt", "x_sample", "cache_sb_k", "cache_sb_v", "state_wkv", "state_shift", "state_conv", "state_pool",
        "norm_g", "ffn_w_gate", "ffn_w_up", "ffn_w_down", "w_in", "w_out", "pool_w", "pool_scale", "rwkv_mu",
        "rwkv_w0", "rwkv_w2", "rwkv_a0", "rwkv_a2", "rwkv_g2", "rwkv_k_k", "rwkv_k_a", "rwkv_r_k", "rwkv_ln_w",
        "rwkv_ln_b", "conv_w"]
_OUTS = [("y_prompt", (1, TP, D)), ("y_sample", (NSTR, TS, D)),
         ("p_sb_k", (DEPTH, 1, TP, NH, HD)), ("p_sb_v", (DEPTH, 1, TP, NH, HD)),
         ("p_wkv", (DEPTH, 1, NH, HD, HD)), ("p_shift", (DEPTH, 1, RWKV_IN)),
         ("p_conv", (DEPTH, 1, CONV_W - 1, G)), ("p_pool", (DEPTH, 1, POOL_ST, G)),
         ("s_sb_k", (DEPTH, NSTR, TS, NH, HD)), ("s_sb_v", (DEPTH, NSTR, TS, NH, HD)),
         ("s_wkv", (DEPTH, NSTR, NH, HD, HD)), ("s_shift", (DEPTH, NSTR, RWKV_IN)),
         ("s_conv", (DEPTH, NSTR, CONV_W - 1, G)), ("s_pool", (DEPTH, NSTR, POOL_ST, G))]


def kernel(**inputs):
    import concourse.bacc as _bacc
    import numpy as _np
    from concourse.bass_utils import run_bass_kernel_spmd as _run

    nc = _bacc.Bacc("TRN2", target_bir_lowering=False, num_devices=1)
    arrays, io = {}, {}
    for name in _INS:
        a = _np.ascontiguousarray(inputs[name])
        arrays[f"in_{name}"] = a
        io[name] = nc.dram_tensor(f"in_{name}", a.shape, mybir.dt.from_np(a.dtype), kind="ExternalInput").ap()
    arrays["in_consts"] = constants(_np)
    io["consts"] = nc.dram_tensor("in_consts", (P, NCON), F32, kind="ExternalInput").ap()
    for name, shape in _OUTS:
        io[name] = nc.dram_tensor(f"out_{name}", shape, F32, kind="ExternalOutput").ap()
    build(nc, io)
    r = _run(nc, [arrays], core_ids=[0])
    return tuple(r.results[0][f"out_{name}"] for name, _ in _OUTS)
```
